# Optimizing a Trainium2 kernel written in Bass

```python
import jax, jax.numpy as jnp
from jax import lax
import numpy as np
import math

D_MODEL = 1024
BATCH = 1
SEQ = 256
DEPTH = 2

HGRN_HEADS = 8
HGRN_EXPAND = 128
HGRN_VDIM = 128
HGRN_KEY_WIDTH = HGRN_HEADS * HGRN_EXPAND
HGRN_VAL_WIDTH = HGRN_HEADS * HGRN_VDIM
HGRN_SCALE = HGRN_EXPAND ** -0.5
CHUNK = 64
F_MIN = 1e-6
CONV_CH = D_MODEL
CONV_K = 3
D_FF = 2816
N_EXPERTS = 8
TOP_K = 2
EPS = 1e-6
N_DENSE = (DEPTH + 1) // 2
N_MOE = DEPTH // 2
IN_SPLITS = (HGRN_KEY_WIDTH, HGRN_KEY_WIDTH, HGRN_VAL_WIDTH, HGRN_VAL_WIDTH,
             CONV_CH, CONV_CH, CONV_CH, D_MODEL, D_MODEL)
IN_WIDTH = sum(IN_SPLITS)


def rms_norm(x, w):
    xf = x.astype(jnp.float32)
    y = xf * lax.rsqrt(jnp.mean(xf * xf, axis=-1, keepdims=True) + EPS)
    return (y * w.astype(jnp.float32)).astype(x.dtype)

def split_projection(h, w):
    outs = []
    start = 0
    for width in IN_SPLITS:
        outs.append(jnp.einsum('bsd,de->bse', h, w[:, start:start + width]))
        start += width
    return outs

def hgrn2_chunk_recurrence(q, k, v, log_f):
    bsz, seq, nh, kd = q.shape
    vd = v.shape[-1]
    n_chunks = seq // CHUNK

    def to_chunks(t):
        return t.reshape(bsz, n_chunks, CHUNK, nh, t.shape[-1]).transpose(1, 0, 3, 2, 4)

    causal = jnp.tril(jnp.ones((CHUNK, CHUNK), dtype=bool))[:, :, None]

    def step(state, inp):
        qc, kc, vc, gc = inp
        cum = jnp.cumsum(gc, axis=2)
        diff = cum[:, :, :, None, :] - cum[:, :, None, :, :]
        decay = jnp.where(causal, jnp.exp(jnp.where(causal, diff, 0.0)), 0.0)
        scores = jnp.einsum('bhtk,bhtsk,bhsk->bhts', qc, decay, kc)
        o = (jnp.einsum('bhts,bhsv->bhtv', scores, vc)
             + jnp.einsum('bhtk,bhkv->bhtv', qc * jnp.exp(cum), state))
        last = cum[:, :, -1:, :]
        state = (jnp.exp(last[:, :, 0, :])[..., None] * state
                 + jnp.einsum('bhsk,bhsv->bhkv', kc * jnp.exp(last - cum), vc))
        return state, o

    s0 = jnp.zeros((bsz, nh, kd, vd), jnp.float32)
    _, o = lax.scan(step, s0, (to_chunks(q), to_chunks(k), to_chunks(v), to_chunks(log_f)))
    return o.transpose(1, 0, 3, 2, 4).reshape(bsz, seq, nh, vd)

def hybrid_mixer(h, w_in, lb, g_norm_w, conv_w, w_proj_hgrn, w_proj_conv, w_out):
    bsz, seq, _ = h.shape
    q, f_logit, i_in, g_out, b_gate, c_gate, u, gate_a, gate_b = split_projection(h, w_in)

    def heads(t):
        return t.reshape(bsz, seq, HGRN_HEADS, -1).astype(jnp.float32)

    z = heads(f_logit)
    lbh = lb.astype(jnp.float32).reshape(HGRN_HEADS, HGRN_EXPAND)
    f = lbh + (1.0 - lbh) * jax.nn.sigmoid(z)
    log_f = jnp.log(jnp.maximum(f, F_MIN))
    k = (1.0 - lbh) * jax.nn.sigmoid(-z)
    qh = jax.nn.silu(heads(q)) * HGRN_SCALE
    o = hgrn2_chunk_recurrence(qh, k, heads(i_in), log_f)
    o = rms_norm(o, g_norm_w) * jax.nn.silu(heads(g_out))
    y_a = jnp.einsum('bse,ed->bsd', o.reshape(bsz, seq, HGRN_VAL_WIDTH).astype(h.dtype), w_proj_hgrn)

    v = b_gate * u
    vp = jnp.pad(v, ((0, 0), (CONV_K - 1, 0), (0, 0)))
    conv = conv_w[0] * vp[:, 0:seq, :]
    for j in range(1, CONV_K):
        conv = conv + conv_w[j] * vp[:, j:j + seq, :]
    y_b = jnp.einsum('bse,ed->bsd', c_gate * conv, w_proj_conv)

    merged = jax.nn.sigmoid(gate_a) * y_a + jax.nn.sigmoid(gate_b) * y_b
    return jnp.einsum('bsd,de->bse', merged, w_out)

def swiglu(h, w1, w3, w2):
    a = jnp.einsum('bsd,df->bsf', h, w1)
    b = jnp.einsum('bsd,df->bsf', h, w3)
    return jnp.einsum('bsf,fd->bsd', jax.nn.silu(a) * b, w2)

def moe_swiglu(h, router_w, w1, w3, w2):
    bsz, seq, d = h.shape
    t = h.reshape(bsz * seq, d)
    logits = jnp.einsum('td,de->te', t, router_w).astype(jnp.float32)
    top_vals, top_idx = lax.top_k(logits, TOP_K)
    top_w = jax.nn.softmax(top_vals, axis=-1)
    gates = jnp.sum(jax.nn.one_hot(top_idx, N_EXPERTS, dtype=jnp.float32) * top_w[..., None], axis=1)
    gates = gates.astype(h.dtype)
    out = jnp.zeros_like(t)
    for e in range(N_EXPERTS):
        a = t @ w1[e]
        b = t @ w3[e]
        out = out + gates[:, e:e + 1] * ((jax.nn.silu(a) * b) @ w2[e])
    return out.reshape(bsz, seq, d)

def first_inputs(seed: int = 0) -> dict:
    key = jax.random.key(seed)
    ks = jax.random.split(key, 20)
    nrm = lambda k, shape, fan_in: jax.random.normal(k, shape, jnp.float32) * (fan_in ** -0.5)
    gain = lambda k, shape: 1.0 + 0.05 * jax.random.normal(k, shape, jnp.float32)
    return {
        "x": jax.random.normal(ks[0], (BATCH, SEQ, D_MODEL), jnp.float32),
        "w_in": nrm(ks[1], (DEPTH, D_MODEL, IN_WIDTH), D_MODEL),
        "lower_bounds": 0.1 * jax.random.normal(ks[2], (DEPTH, HGRN_KEY_WIDTH), jnp.float32),
        "hgrn_norm_w": gain(ks[3], (DEPTH, HGRN_VDIM)),
        "conv_w": nrm(ks[4], (DEPTH, CONV_K, CONV_CH), CONV_K),
        "w_proj_hgrn": nrm(ks[5], (DEPTH, HGRN_VAL_WIDTH, D_MODEL), HGRN_VAL_WIDTH),
        "w_proj_conv": nrm(ks[6], (DEPTH, CONV_CH, D_MODEL), CONV_CH),
        "w_out": nrm(ks[7], (DEPTH, D_MODEL, D_MODEL), D_MODEL),
        "norm_mix": gain(ks[8], (DEPTH, D_MODEL)),
        "norm_ffn": gain(ks[9], (DEPTH, D_MODEL)),
        "dense_w1": nrm(ks[10], (N_DENSE, D_MODEL, D_FF), D_MODEL),
        "dense_w3": nrm(ks[11], (N_DENSE, D_MODEL, D_FF), D_MODEL),
        "dense_w2": nrm(ks[12], (N_DENSE, D_FF, D_MODEL), D_FF),
        "router_w": nrm(ks[13], (N_MOE, D_MODEL, N_EXPERTS), D_MODEL),
        "expert_w1": nrm(ks[14], (N_MOE, N_EXPERTS, D_MODEL, D_FF), D_MODEL),
        "expert_w3": nrm(ks[15], (N_MOE, N_EXPERTS, D_MODEL, D_FF), D_MODEL),
        "expert_w2": nrm(ks[16], (N_MOE, N_EXPERTS, D_FF, D_MODEL), D_FF),
        "final_norm": gain(ks[17], (D_MODEL,)),
    }

def first_block(x, w_in, lower_bounds, hgrn_norm_w, conv_w, w_proj_hgrn, w_proj_conv, w_out,
              norm_mix, norm_ffn, dense_w1, dense_w3, dense_w2, router_w,
              expert_w1, expert_w3, expert_w2, final_norm):
    lb_soft = jax.nn.softmax(lower_bounds.astype(jnp.float32), axis=0)
    lb_all = jnp.cumsum(lb_soft, axis=0) - lb_soft[0]
    for layer in range(DEPTH):
        h = rms_norm(x, norm_mix[layer])
        x = x + hybrid_mixer(h, w_in[layer], lb_all[layer], hgrn_norm_w[layer], conv_w[layer],
                             w_proj_hgrn[layer], w_proj_conv[layer], w_out[layer])
        h = rms_norm(x, norm_ffn[layer])
        if layer % 2 == 0:
            j = layer // 2
            x = x + swiglu(h, dense_w1[j], dense_w3[j], dense_w2[j])
        else:
            j = layer // 2
            x = x + moe_swiglu(h, router_w[j], expert_w1[j], expert_w3[j], expert_w2[j])
    return rms_norm(x, final_norm)


HEAD_DIM = 64
ROT_DIM = HEAD_DIM // 4
ROPE_THETA = 500000.0
Q_BLOCK = 128
NEG = -1e30
PLE_DIM = 256

DA_HEADS = 4
DA_QK = DA_HEADS * 2 * HEAD_DIM
DA_VDIM = 2 * HEAD_DIM
DA_WIDTH = DA_HEADS * DA_VDIM

DSA_HEADS = 8
DSA_WIDTH = DSA_HEADS * HEAD_DIM
IDX_HEADS = 8
IDX_DIM = 64
DSA_TOPK_MAX = 256

NSA_GROUPS = 2
NSA_HPG = 4
NSA_HEADS = NSA_GROUPS * NSA_HPG
NSA_WIDTH = NSA_HEADS * HEAD_DIM
KV_C = NSA_GROUPS * HEAD_DIM
CMP_LEN = 32
CMP_STRIDE = 16
CMP_HIDDEN = 128
SLC_BLOCK = 64
SLC_TOPN_MAX = 16
WINDOW = 512
FORCE_SCORE = 1e4

BRANCH_WIDTH = 512
N_BRANCH = 3

IN_SPLITS_2 = (
    DA_QK, DA_QK, DA_WIDTH, BRANCH_WIDTH,
    DSA_WIDTH, HEAD_DIM, HEAD_DIM, BRANCH_WIDTH,
    IDX_HEADS * IDX_DIM, IDX_DIM, IDX_HEADS,
    NSA_WIDTH, KV_C, KV_C, KV_C, KV_C, KV_C, KV_C,
    BRANCH_WIDTH, NSA_HEADS * 3,
    N_BRANCH * D_MODEL,
)
N_IN = sum(IN_SPLITS_2)


def rmsnorm(x, g):
    xf = x.astype(jnp.float32)
    y = xf * lax.rsqrt(jnp.mean(xf * xf, axis=-1, keepdims=True) + EPS)
    return (y * g.astype(jnp.float32)).astype(x.dtype)

def masked_softmax(s, mask):
    s = jnp.where(mask, s.astype(jnp.float32), NEG)
    return jnp.where(mask, jax.nn.softmax(s, axis=-1), 0.0)

def rope_tables(positions):
    inv = ROPE_THETA ** (-jnp.arange(0, ROT_DIM, 2, dtype=jnp.float32) / ROT_DIM)
    ang = positions.astype(jnp.float32)[..., None] * inv
    return jnp.cos(ang), jnp.sin(ang)

def apply_rope(x, cos, sin):
    shp = cos.shape[:2] + (1,) * (x.ndim - 3) + cos.shape[2:]
    c = cos.reshape(shp).astype(x.dtype)
    s = sin.reshape(shp).astype(x.dtype)
    half = ROT_DIM // 2
    x1, x2 = x[..., :half], x[..., half:ROT_DIM]
    return jnp.concatenate([x1 * c - x2 * s, x2 * c + x1 * s, x[..., ROT_DIM:]], axis=-1)

def unblock(o):
    nb, b, qb = o.shape[:3]
    return jnp.moveaxis(o, 0, 1).reshape(b, nb * qb, -1)

def diff_attention(q, k, v, lam, subln_g, lam_init):
    S = q.shape[1]
    kpos = jnp.arange(S)
    scale = HEAD_DIM ** -0.5

    def block(i):
        q0 = i * Q_BLOCK
        tpos = q0 + jnp.arange(Q_BLOCK)
        qb = lax.dynamic_slice_in_dim(q, q0, Q_BLOCK, axis=1)
        s = jnp.einsum('bqhcd,bkhcd->bhcqk', qb, k).astype(jnp.float32) * scale
        pr = masked_softmax(s, kpos[None, :] <= tpos[:, None])
        a = pr[:, :, 0] - lam * pr[:, :, 1]
        return jnp.einsum('bhqk,bkhe->bqhe', a.astype(v.dtype), v)

    o = lax.map(block, jnp.arange(S // Q_BLOCK))
    b = q.shape[0]
    o = jnp.moveaxis(o, 0, 1).reshape(b, S, DA_HEADS, DA_VDIM)
    o = rmsnorm(o, subln_g) * (1.0 - lam_init)
    return o.reshape(b, S, DA_WIDTH)

def dsa_attention(q, k, v, iq, ik, iw, k_sel):
    S = q.shape[1]
    kpos = jnp.arange(S)
    scale = HEAD_DIM ** -0.5
    gather = jax.vmap(lambda kk, ii: kk[ii])

    def block(i):
        q0 = i * Q_BLOCK
        tpos = q0 + jnp.arange(Q_BLOCK)
        qb = lax.dynamic_slice_in_dim(q, q0, Q_BLOCK, axis=1)
        iqb = lax.dynamic_slice_in_dim(iq, q0, Q_BLOCK, axis=1)
        iwb = lax.dynamic_slice_in_dim(iw, q0, Q_BLOCK, axis=1).astype(jnp.float32) * IDX_HEADS ** -0.5
        dots = jnp.einsum('bqhd,bkd->bqhk', iqb, ik).astype(jnp.float32) * IDX_DIM ** -0.5
        score = jnp.einsum('bqh,bqhk->bqk', iwb, jax.nn.relu(dots))
        score = jnp.where(kpos[None, :] <= tpos[:, None], score, -jnp.inf)
        _, idx = lax.top_k(score, k_sel)
        valid = idx <= tpos[None, :, None]
        ksel = gather(k, idx)
        vsel = gather(v, idx)
        s = jnp.einsum('bqhd,bqkd->bqhk', qb, ksel).astype(jnp.float32) * scale
        pr = masked_softmax(s, valid[:, :, None, :])
        return jnp.einsum('bqhk,bqkd->bqhd', pr.astype(v.dtype), vsel)

    return unblock(lax.map(block, jnp.arange(S // Q_BLOCK)))

def compress(kv, pe, w1, w2):
    S = kv.shape[1]
    nc = (S - CMP_LEN) // CMP_STRIDE + 1
    idx = np.arange(nc)[:, None] * CMP_STRIDE + np.arange(CMP_LEN)[None, :]
    blocks = kv[:, idx] + pe[None, None, :, None, :]
    hid = jax.nn.gelu(jnp.einsum('bnlgd,ldf->bngf', blocks, w1))
    return jnp.einsum('bngf,fd->bngd', hid, w2)

def nsa_attention(q, q_rot, kc, vc, ks, vs, kw, vw, gates, n_sel):
    B, S = q.shape[:2]
    nc = kc.shape[1]
    n_blk = S // SLC_BLOCK
    scale = HEAD_DIM ** -0.5
    cstart = np.arange(nc) * CMP_STRIDE
    sstart = np.arange(n_blk) * SLC_BLOCK
    overlap = jnp.asarray(((cstart[:, None] < sstart[None, :] + SLC_BLOCK)
                           & (cstart[:, None] + CMP_LEN > sstart[None, :])).astype(np.float32))
    cmp_end = jnp.arange(nc) * CMP_STRIDE + CMP_LEN - 1
    blk = jnp.arange(n_blk)
    ks_blk = ks.reshape(B, n_blk, SLC_BLOCK, NSA_GROUPS, HEAD_DIM).transpose(0, 3, 1, 2, 4)
    vs_blk = vs.reshape(B, n_blk, SLC_BLOCK, NSA_GROUPS, HEAD_DIM).transpose(0, 3, 1, 2, 4)
    kw_pad = jnp.pad(kw, ((0, 0), (WINDOW, 0), (0, 0), (0, 0)))
    vw_pad = jnp.pad(vw, ((0, 0), (WINDOW, 0), (0, 0), (0, 0)))
    gather = jax.vmap(jax.vmap(lambda kb, ii: kb[ii]))

    def block(i):
        q0 = i * Q_BLOCK
        tpos = q0 + jnp.arange(Q_BLOCK)
        qb = lax.dynamic_slice_in_dim(q, q0, Q_BLOCK, axis=1)
        qrb = lax.dynamic_slice_in_dim(q_rot, q0, Q_BLOCK, axis=1)
        gb = jax.nn.sigmoid(lax.dynamic_slice_in_dim(gates, q0, Q_BLOCK, axis=1))
        sc = jnp.einsum('bqghd,bngd->bghqn', qb, kc).astype(jnp.float32) * scale
        pc = masked_softmax(sc, cmp_end[None, :] <= tpos[:, None])
        o_cmp = jnp.einsum('bghqn,bngd->bqghd', pc.astype(vc.dtype), vc)
        imp = jnp.einsum('bghqn,nm->bgqm', pc, overlap)
        forced = (blk[None, :] == (tpos // SLC_BLOCK)[:, None]) | (blk[None, :] == 0)
        imp = jnp.where(forced, FORCE_SCORE, imp)
        imp = jnp.where(blk[None, :] * SLC_BLOCK <= tpos[:, None], imp, -jnp.inf)
        _, sel = lax.top_k(imp, n_sel)
        ksel = gather(ks_blk, sel)
        vsel = gather(vs_blk, sel).reshape(B, NSA_GROUPS, Q_BLOCK, n_sel * SLC_BLOCK, HEAD_DIM)
        spos = sel[..., None] * SLC_BLOCK + jnp.arange(SLC_BLOCK)
        smask = (spos <= tpos[:, None, None]).reshape(B, NSA_GROUPS, Q_BLOCK, n_sel * SLC_BLOCK)
        ss = jnp.einsum('bqghd,bgqnjd->bghqnj', qrb, ksel).astype(jnp.float32) * scale
        ps = masked_softmax(ss.reshape(B, NSA_GROUPS, NSA_HPG, Q_BLOCK, n_sel * SLC_BLOCK), smask[:, :, None])
        o_slc = jnp.einsum('bghqk,bgqkd->bqghd', ps.astype(vsel.dtype), vsel)
        kwb = lax.dynamic_slice_in_dim(kw_pad, q0, Q_BLOCK + WINDOW, axis=1)
        vwb = lax.dynamic_slice_in_dim(vw_pad, q0, Q_BLOCK + WINDOW, axis=1)
        wpos = q0 - WINDOW + jnp.arange(Q_BLOCK + WINDOW)
        wmask = ((wpos[None, :] <= tpos[:, None]) & (wpos[None, :] > tpos[:, None] - WINDOW)
                 & (wpos[None, :] >= 0))
        sw = jnp.einsum('bqghd,bkgd->bghqk', qrb, kwb).astype(jnp.float32) * scale
        pw = masked_softmax(sw, wmask)
        o_win = jnp.einsum('bghqk,bkgd->bqghd', pw.astype(vwb.dtype), vwb)
        return gb[..., 0:1] * o_cmp + gb[..., 1:2] * o_slc + gb[..., 2:3] * o_win

    return unblock(lax.map(block, jnp.arange(S // Q_BLOCK)))

def second_inputs(seed: int = 0) -> dict:
    key = jax.random.key(seed)
    ks = jax.random.split(key, 20)

    def nrm(k, shape, scale):
        return jax.random.normal(k, shape, jnp.float32) * scale

    L, D = DEPTH, D_MODEL
    return {
        "x": nrm(ks[0], (BATCH, SEQ, D), 1.0),
        "p": nrm(ks[1], (DEPTH, BATCH, SEQ, PLE_DIM), 1.0),
        "positions": jnp.broadcast_to(jnp.arange(SEQ, dtype=jnp.int32)[None, :], (BATCH, SEQ)),
        "norm_g": 1.0 + nrm(ks[2], (L, D), 0.02),
        "w_in": nrm(ks[3], (L, D, N_IN), D ** -0.5),
        "diff_lambda": nrm(ks[4], (L, 4, HEAD_DIM), 0.1),
        "diff_subln_g": 1.0 + nrm(ks[5], (L, DA_VDIM), 0.02),
        "cmp_pe_k": nrm(ks[6], (L, CMP_LEN, HEAD_DIM), 0.1),
        "cmp_w1_k": nrm(ks[7], (L, CMP_LEN, HEAD_DIM, CMP_HIDDEN), (CMP_LEN * HEAD_DIM) ** -0.5),
        "cmp_w2_k": nrm(ks[8], (L, CMP_HIDDEN, HEAD_DIM), CMP_HIDDEN ** -0.5),
        "cmp_pe_v": nrm(ks[9], (L, CMP_LEN, HEAD_DIM), 0.1),
        "cmp_w1_v": nrm(ks[10], (L, CMP_LEN, HEAD_DIM, CMP_HIDDEN), (CMP_LEN * HEAD_DIM) ** -0.5),
        "cmp_w2_v": nrm(ks[11], (L, CMP_HIDDEN, HEAD_DIM), CMP_HIDDEN ** -0.5),
        "w_up": nrm(ks[12], (L, N_BRANCH, BRANCH_WIDTH, D), BRANCH_WIDTH ** -0.5),
        "w_out": nrm(ks[13], (L, D, D), D ** -0.5),
        "ple_norm_g": 1.0 + nrm(ks[14], (L, D), 0.02),
        "w_ple": nrm(ks[15], (L, PLE_DIM, D), PLE_DIM ** -0.5),
        "w_ple_gate": nrm(ks[16], (L, D, D), D ** -0.5),
        "final_norm_g": 1.0 + nrm(ks[17], (D,), 0.02),
    }

def second_block(x, p, positions, norm_g, w_in, diff_lambda, diff_subln_g,
              cmp_pe_k, cmp_w1_k, cmp_w2_k, cmp_pe_v, cmp_w1_v, cmp_w2_v,
              w_up, w_out, ple_norm_g, w_ple, w_ple_gate, final_norm_g):
    B, S, D = x.shape
    k_sel = min(DSA_TOPK_MAX, S // 4)
    n_sel = min(SLC_TOPN_MAX, S // SLC_BLOCK)
    cos, sin = rope_tables(positions)
    offsets = np.cumsum(IN_SPLITS_2)[:-1].tolist()
    for i in range(DEPTH):
        h = rmsnorm(x, norm_g[i])
        z = h @ w_in[i]
        (a_q, a_k, a_v, a_g, b_q, b_k, b_v, b_g, i_q, i_k, i_w,
         c_q, c_kc, c_vc, c_ks, c_vs, c_kw, c_vw, c_g, c_bg, merge) = jnp.split(z, offsets, axis=-1)

        lam_init = 0.8 - 0.6 * math.exp(-0.3 * i)
        lp = diff_lambda[i].astype(jnp.float32)
        lam = jnp.exp(jnp.sum(lp[0] * lp[1])) - jnp.exp(jnp.sum(lp[2] * lp[3])) + lam_init
        qa = apply_rope(a_q.reshape(B, S, DA_HEADS, 2, HEAD_DIM), cos, sin)
        ka = apply_rope(a_k.reshape(B, S, DA_HEADS, 2, HEAD_DIM), cos, sin)
        o_a = diff_attention(qa, ka, a_v.reshape(B, S, DA_HEADS, DA_VDIM), lam, diff_subln_g[i], lam_init)

        o_b = dsa_attention(apply_rope(b_q.reshape(B, S, DSA_HEADS, HEAD_DIM), cos, sin),
                            apply_rope(b_k, cos, sin), b_v,
                            apply_rope(i_q.reshape(B, S, IDX_HEADS, IDX_DIM), cos, sin),
                            apply_rope(i_k, cos, sin), i_w, k_sel)

        grp = (B, S, NSA_GROUPS, HEAD_DIM)
        qc = c_q.reshape(B, S, NSA_GROUPS, NSA_HPG, HEAD_DIM)
        kc = compress(c_kc.reshape(grp), cmp_pe_k[i], cmp_w1_k[i], cmp_w2_k[i])
        vc = compress(c_vc.reshape(grp), cmp_pe_v[i], cmp_w1_v[i], cmp_w2_v[i])
        o_c = nsa_attention(qc, apply_rope(qc, cos, sin), kc, vc,
                            apply_rope(c_ks.reshape(grp), cos, sin), c_vs.reshape(grp),
                            apply_rope(c_kw.reshape(grp), cos, sin), c_vw.reshape(grp),
                            c_bg.reshape(B, S, NSA_GROUPS, NSA_HPG, 3), n_sel)

        branches = jnp.stack([o_a * jax.nn.silu(a_g), o_b * jax.nn.silu(b_g),
                              o_c * jax.nn.silu(c_g)], axis=2)
        up = jnp.einsum('bsnw,nwd->bsnd', branches, w_up[i])
        gates = jax.nn.sigmoid(merge.reshape(B, S, N_BRANCH, D))
        x = x + jnp.sum(gates * up, axis=2) @ w_out[i]

        x = x + (p[i] @ w_ple[i]) * jax.nn.sigmoid(rmsnorm(x, ple_norm_g[i]) @ w_ple_gate[i])
    return rmsnorm(x, final_norm_g)


def setup_inputs(seed=0):
    out = dict(first_inputs(seed))
    for name, value in second_inputs(seed + 1).items():
        if name != "x":
            out[name + "_2"] = value
    return out


def reference(
    x, w_in, lower_bounds, hgrn_norm_w, conv_w, w_proj_hgrn, w_proj_conv, w_out, norm_mix,
    norm_ffn, dense_w1, dense_w3, dense_w2, router_w, expert_w1, expert_w3, expert_w2,
    final_norm, p_2, positions_2, norm_g_2, w_in_2, diff_lambda_2, diff_subln_g_2, cmp_pe_k_2,
    cmp_w1_k_2, cmp_w2_k_2, cmp_pe_v_2, cmp_w1_v_2, cmp_w2_v_2, w_up_2, w_out_2, ple_norm_g_2,
    w_ple_2, w_ple_gate_2, final_norm_g_2,
):
    x = first_block(
        x, w_in, lower_bounds, hgrn_norm_w, conv_w, w_proj_hgrn, w_proj_conv, w_out, norm_mix,
        norm_ffn, dense_w1, dense_w3, dense_w2, router_w, expert_w1, expert_w3, expert_w2,
        final_norm,
    )
    return second_block(
        x, p_2, positions_2, norm_g_2, w_in_2, diff_lambda_2, diff_subln_g_2, cmp_pe_k_2,
        cmp_w1_k_2, cmp_w2_k_2, cmp_pe_v_2, cmp_w1_v_2, cmp_w2_v_2, w_up_2, w_out_2,
        ple_norm_g_2, w_ple_2, w_ple_gate_2, final_norm_g_2,
    )


_drawn_inputs = setup_inputs


def setup_inputs(seed=0):
    import zlib

    import numpy as np

    out = dict(_drawn_inputs(seed))
    spreads = {}
    factors = {'lower_bounds': 4.711,
     'norm_g_2': 3.622,
     'diff_lambda_2': 3.309,
     'diff_subln_g_2': 8.0,
     'cmp_pe_k_2': 8.0,
     'cmp_pe_v_2': 4.64,
     'ple_norm_g_2': 70.36,
     'final_norm_g_2': 22.705}
    for name, (base, spread) in spreads.items():
        noise = np.random.default_rng([zlib.crc32(name.encode()), seed]).standard_normal(out[name].shape)
        drawn = base * np.exp(spread * noise) if base else spread * noise
        out[name] = __import__('jax').numpy.asarray(drawn.astype(out[name].dtype))
    for name, factor in factors.items():
        out[name] = (out[name] * factor).astype(out[name].dtype)
    return out
```

```python
import math
from contextlib import ExitStack

import numpy as np

import concourse.bass as bass
from concourse import mybir

F32 = mybir.dt.float32
I32 = mybir.dt.int32
ALU = mybir.AluOpType
ACT = mybir.ActivationFunctionType
AX_X = mybir.AxisListType.X

P = 128
T = 256
TH = T // P
D = 1024
KD = D // P
W = 512
NP = 9
PAGE = 2048
EPS = 1e-6
NEG = -1e30
TAKEN = -3e38

HEADS = 8
CH = 64
NC = T // CH
SUB = 8
NSUB = CH // SUB
F_MIN = 1e-6
D_FF = 2816
STEPS = D_FF // 256
EXPERTS = 8

HD = 64
SCALE = HD ** -0.5
ROT = 8
THETA = 500000.0
K_SEL = 64
NCMP = 15
Z_COLS = 5600
A_Q, A_V, A_G = 0, 1024, 1536
B_Q, B_K, B_V, B_G = 2048, 2560, 2624, 2688
I_Q, I_K, I_W = 3200, 3712, 3776
C_Q, C_KC, C_VC, C_KS, C_VS, C_KW, C_VW = 3784, 4296, 4424, 4552, 4680, 4808, 4936
C_G, C_BG = 5064, 5576
T_AQ, T_AK, T_BQ, T_IQ, T_CQ, T_CR, T_BK, T_IK, T_KS, T_KW, T_KC, T_VC = 0, 4, 8, 12, 16, 20, 24, 25, 26, 28, 30, 31


N_PARAMS = 25
N_CONSTS = 9
TILES_1 = 44
ROUND = 1.5 * 2 ** 23
PI2 = (6.28125, 0.0019350051879882812, 3.019916e-7)
PI_UP = 3.1415925
ATT = 10
PAGES_FFN = 3 * STEPS

NAMES = """params consts act_step dve_step pool_step x_ready squares variance deviation h_scaled hT_psum hT_ready
used tile_evac f_sig z_sig q_sig f_ready log_f shifted_q exp_q qa_on ka_zero shifted_k exp_k ka_on scores_on s_masked
exp_cum exp_last shifted_l exp_l kl_on klt_psum klt_sb u_on states_on qe_on o_psum o_act o_dve silu_g o_on oT_psum oT_sb
conv_ready gates_on merged x_full silu_on hid_on y_added logits top_diff top_exp row_in out_done rope_on qT_psum qT_act
qT_dve pe_psum cmp_in cmp_peT cmp_x gelu_on cmp_out cmp_sb dots_full relu_on relu_read scores_full scores_cut exp_on
pT_psum pT_act pT_dve av_full attn_out cs_full cs_cut cs_exp cs_norm pcT_psum pcT_sb cav_full branch_gates branch_on
bT_psum bT_act bT_dve up_merged p_in pT2_psum pT2_sb sub_var sub_dev init_act init_dve angles tables hidc_on lg_read lam_sum lam_exp lb_max sub2_var sub2_dev""" 


def ffn_page(j, part):
    if part < 2:
        return part if j == 0 else 3 * j - 1 + part
    return 3 * j + 4 if j < STEPS - 1 else PAGES_FFN - 1


class Ring:

    def __init__(self):
        self.seq = 0
        self.fills = [0] * NP
        self.extra = [0] * NP
        self.last = [0] * NP

    def at(self, k, i, pages):
        p = k % NP
        return p, self.fills[p] + k // NP + i * ((pages - p + NP - 1) // NP)

    def free(self, k, i, pages):
        if k >= NP:
            return self.seq + i * pages + k - NP + 1
        if isinstance(i, int) and i == 0:
            return self.last[k]
        return self.seq + (i - 1) * pages + (pages - 1 - k) // NP * NP + k + 1

    def close(self, pages, turns=1, dmas=1):
        for p in range(min(NP, pages)):
            per = (pages - p + NP - 1) // NP
            self.fills[p] += per * turns
            self.extra[p] += 16 * (dmas - 1) * per * turns
            self.last[p] = self.seq + (turns - 1) * pages + (pages - 1 - p) // NP * NP + p + 1
        self.seq += pages * turns


def build(nc, A, out, stop=99):
    ctx = ExitStack()
    with ctx:
        def sb(name, shape, dt=F32):
            return ctx.enter_context(nc.sbuf_tensor(name, shape, dt))[:]

        def sem(name):
            return ctx.enter_context(nc.semaphore(name))

        ring = sb("ring", [P, NP, PAGE])
        x = sb("x_tok", [P, TH, D])
        hT = sb("hT", [P, KD, T])
        htok = sb("htok", [P, TH, D])
        AR = sb("arena", [P, 27136])

        def area(at, *shape):
            n = 1
            for s in shape:
                n *= s
            v = AR[:, at:at + n]
            if len(shape) == 1:
                return v
            if len(shape) == 2:
                return v.rearrange("p (a b) -> p a b", b=shape[1])
            return v.rearrange("p (a b c) -> p a b c", b=shape[1], c=shape[2])

        zF = area(0, 56, T)
        zT = area(14336, TH, 2048)
        bF = area(18432, 2048)
        bC = area(20480, 2048)
        bQ = area(22528, 2048)
        bK = area(24576, 2048)
        sil = area(0, 2, 512)
        hid = area(1024, 2, 512)
        zt = area(0, TH, Z_COLS)
        QT = area(11200, 32, T)
        zm = area(19392, 24, T)
        kdup = area(25536, TH, 6, P)
        osum = area(25536, 8, P)
        cx = area(25536, 4, T)
        crt = htok[:].rearrange("p h d -> p (h d)")[:, 0:1024].rearrange("p (h d) -> p h d", h=TH)
        sv = htok[:].rearrange("p h (s k) -> p (h s) k", k=T)
        PT = hT[:].rearrange("p (b s) (u q) -> p b (s u) q", b=2, u=2)
        PL = area(0, TH, T)
        pTs = area(512, 2, T)
        pl = area(1024, TH, D)
        plg = area(3072, TH, D)
        frow = area(6144, D)
        sTm = sb("scoresT", [P, 16, CH])
        sTf = sTm[:].rearrange("p s t -> p (s t)")
        score, work, bias = sTf[:, 0:T], sTf[:, T:2 * T], sTf[:, 2 * T:3 * T]
        pe_t, w2k = sTf[:, 3 * T:3 * T + P], sTf[:, 3 * T + P:4 * T]

        ident = sb("ident", [P, P])
        caus = sb("caus", [P, P])
        cmask = sb("cmask", [P, TH, 16])
        cm01 = sb("cm01", [P, TH, 16])
        smask = sb("smask", [P, CH], I32)
        ones = sb("ones", [P, T])
        reset = sb("reset", [P, T])
        gains = sb("gains", [P, 8, KD])
        lbr = sb("lbr", [P, 2, KD])
        lbt = sb("lbt", [P, 6, KD])
        lbT = sb("lbT", [P, 2, KD])
        oml = sb("oml", [P, 2, KD])
        cw = sb("cw", [P, 2, 3, KD])
        gn = sb("gn", [P, 2, P])
        sg2 = sb("sg2", [P, 2, P])
        lams = sb("lams", [P, 8])
        nlam = sb("nlam", [P, 2])
        posi = sb("posi", [P, TH], I32)
        posf = sb("posf", [P, TH])
        inv = sb("inv", [P, ROT])
        ang = sb("ang", [P, TH, ROT])
        rr = sb("rr", [P, 2 * TH, ROT])
        tq = sb("tq", [P, TH, ROT])
        cosb = sb("cosb", [P, TH, ROT])
        sinb = sb("sinb", [P, TH, ROT])
        rt = sb("rt", [P, 4, TH * 16 * ROT])
        lamr = rt[:, 0:2, :]
        router = sb("router", [P, KD, EXPERTS])
        st = sb("st", [P, 16])
        hst = sb("hst", [P, 16])
        hst2 = sb("hst2", [P, 16])
        eL = sb("eL", [P, 32])
        mx = sb("mx", [P, 8])
        den = sb("den", [P, 8])
        rden = sb("rden", [P, 8])
        m8 = sb("m8", [P, 8])
        iws = sb("iws", [P, TH, 8])
        bgs = sb("bgs", [P, TH, 24])
        peT = sb("peT", [P, 2, 32])
        gel = sb("gel", [P, 4, 16])
        hidc = sb("hidc", [P, 2, P])
        w2v = sb("w2v", [P, HD])
        kcT = sb("kcT", [P, 2, 16])
        vcr = sb("vcr", [P, 2, HD])
        pc = sb("pc", [P, 8, 32])
        pcT = sb("pcT", [P, 2, P])
        lg = sb("lg", [P, 10, 8])
        gate = sb("gate", [P, TH, 8])

        psG = ctx.enter_context(nc.psum_tensor("psG", [P, 2, 2, 512], F32))
        psX = ctx.enter_context(nc.psum_tensor("psX", [P, 4, 512], F32))

        landed = [sem(f"landed{p}") for p in range(NP)]
        S = {n: sem(n) for n in NAMES.split()}
        params, used = S["params"], S["used"]
        block = ctx.enter_context(nc.Block())

        def bc(ap, *shape):
            return ap.to_broadcast([ap.shape[0], *shape])

        def hc(b):
            return b.rearrange("p (h t) -> p h t", t=CH)

        def hd(b):
            return b.rearrange("p (h t) -> p h t", t=T)

        psGf = psG[:].rearrange("p a b c -> p a (b c)")
        psXc = psX[:].rearrange("p b (c t) -> p (b c) t", t=T)
        psXs = psX[:, 0:2, :].rearrange("p b (s t) -> p (b s) t", t=CH)
        psG4 = psG[:, 0, :, :].rearrange("p b (c t) -> p (b c) t", t=T)
        htok_f = htok[:].rearrange("p h d -> p (h d)")
        o_tok = bK.rearrange("p (h d) -> p h d", h=TH)
        states = [None] + [v.rearrange("p (h d) -> p h d", d=P) for v in (bC[:, 0:1024], bC[:, 1024:2048], htok_f[:, 0:1024])]
        hid4 = hid.rearrange("p b (k t) -> p b k t", k=2)
        kdf = kdup.rearrange("p h w d -> p h (w d)")
        pcf = pc[:].rearrange("p s n -> p (s n)")
        oTv = hd(bQ)
        w_q, w_k, w_b, w_c, w_u = (zF[:, 8 * n:8 * n + 8, :] for n in (0, 1, 2, 3, 4))

        def heads_of(kind, p, c):
            g = c // 2
            return {"A": (T_AQ + c, T_AK + c), "B": (T_BQ + c, T_BK), "I": (T_IQ + c, T_IK),
                    "S": (T_CR + c, T_KS + g), "W": (T_CR + c, T_KW + g), "C": (T_CQ + c, None)}[kind]

        @block.sync
        def _(sp):
            count = [0]

            def small(dst, src):
                sp.dma_start(dst, src).then_inc(params, 16)
                count[0] += 1

            R = Ring()

            def load(k, i, pages, src, cols):
                p, _ = R.at(k, i, pages)
                free = R.free(k, i, pages)
                if not (isinstance(free, int) and free == 0):
                    sp.wait_ge(used, free)
                dst = ring[:, p, 0:src.shape[1] * cols].rearrange("p (a b) -> p a b", b=cols)
                sp.dma_start(dst, src).then_inc(landed[p], 16)

            def rows(w):
                return w.rearrange("(k p) n -> p k n", p=P)

            def project(k, i, pages, w, col, cols=W):
                for h in range(2):
                    load(k + h, i, pages, rows(w)[:, 4 * h:4 * h + 4, bass.ds(col, cols)], cols)

            def ffn(w1, w3, w2, i):
                for j in range(STEPS + 1):
                    if j < STEPS:
                        load(ffn_page(j, 0), i, PAGES_FFN, w1[:, :, 256 * j:256 * j + 256], 256)
                        load(ffn_page(j, 1), i, PAGES_FFN, w3[:, :, 256 * j:256 * j + 256], 256)
                    if j:
                        load(ffn_page(j - 1, 2), i, PAGES_FFN, w2[:, 2 * j - 2:2 * j, :], D)

            def first_layer(l):
                w = A["w_in"][l]
                for t in range(4):
                    project(2 * t, 0, 8, w, W * t)
                R.close(8)
                for t in range(4):
                    project(2 * t, 0, 8, w, 2048 + W * t)
                R.close(8)
                for i in range(2):
                    for t in range(4):
                        project(2 * t, i, 8, w, 4096 + 2048 * i + W * t)
                R.close(8, 2)
                for t in range(2):
                    project(2 * t, 0, 4, w, 8192 + W * t)
                R.close(4)
                for t in range(2):
                    project(2 * t, 0, 8, A["w_proj_hgrn"][l], W * t)
                for t in range(2):
                    project(2 * t + 4, 0, 8, A["w_proj_conv"][l], W * t)
                R.close(8)
                for t in range(2):
                    project(2 * t, 0, 4, A["w_out"][l], W * t)
                R.close(4)
                if l == 0:
                    ffn(rows(A["dense_w1"][0]), rows(A["dense_w3"][0]), rows(A["dense_w2"][0]), 0)
                    R.close(PAGES_FFN)
                else:
                    def expert(e):
                        ffn(*[A[w][0, bass.ds(e, 1)].rearrange("o (k p) n -> p (o k) n", p=P)
                              for w in ("expert_w1", "expert_w3", "expert_w2")], e)

                    expert(0)
                    with sp.Fori(1, EXPERTS) as e:
                        expert(e)
                    R.close(PAGES_FFN, EXPERTS)

            def second_layer(l):
                w = A["w_in_2"][l]
                for i in range(2):
                    for t in range(4):
                        project(2 * t, i, 8, w, 2048 * i + W * t)
                R.close(8, 2)
                for t in range(3):
                    project(2 * t, 0, 6, w, 4096 + W * t, min(W, Z_COLS - 4096 - W * t))
                R.close(6)
                for g in range(2):
                    for t in range(3):
                        project(2 * t, 0, 6, w, Z_COLS + 1536 * g + W * t)
                    R.close(6)
                if l:
                    sp.wait_ge(S["cmp_sb"], 2 * l)
                for g in range(2):
                    sp.dma_start(w2k[:, 64 * g:64 * g + 64], A["cmp_w2_k_2"][l]).then_inc(S["cmp_in"], 16)
                    sp.dma_start(pe_t[0:32, 64 * g:64 * g + 64], A["cmp_pe_k_2"][l]).then_inc(S["cmp_in"], 16)
                    sp.dma_start(pe_t[32:64, 64 * g:64 * g + 64], A["cmp_pe_v_2"][l]).then_inc(S["cmp_in"], 16)
                sp.dma_start(w2v[:], A["cmp_w2_v_2"][l]).then_inc(S["cmp_in"], 16)
                for n, name in enumerate(("cmp_w1_k_2", "cmp_w1_v_2")):
                    for h in range(2):
                        p, _ = R.at(2 * n + h, 0, 4)
                        sp.wait_ge(used, R.free(2 * n + h, 0, 4))
                        for g in range(2):
                            sp.dma_start(ring[64 * g:64 * g + 64, p, :].rearrange("p (a b) -> p a b", b=P),
                                         A[name][l, 16 * h:16 * h + 16].rearrange("l d f -> d l f")).then_inc(landed[p], 16)
                R.close(4, 1, 2)
                for b in range(3):
                    for t in range(2):
                        load(2 * b + t, 0, 6, rows(A["w_up_2"][l, b])[:, :, W * t:W * t + W], W)
                R.close(6)
                for t in range(2):
                    project(2 * t, 0, 4, A["w_out_2"][l], W * t)
                R.close(4)
                load(0, 0, 1, rows(A["w_ple_2"][l]), D)
                R.close(1)
                for t in range(2):
                    project(2 * t, 0, 4, A["w_ple_gate_2"][l], W * t)
                R.close(4)

            def row(name, m):
                sp.wait_ge(S["x_ready"], m)
                sp.dma_start(frow, A[name].rearrange("(o d) -> o d", o=1).to_broadcast([P, D])).then_inc(S["row_in"], 16)

            with nc.allow_non_contiguous_dma(reason="gains by feature, a few thousand elements once"):
                small(x[:], A["x"][0].rearrange("(h p) d -> p h d", p=P))
                for l in range(2):
                    for n, name in enumerate(("norm_mix", "norm_ffn", "norm_g_2", "ple_norm_g_2")):
                        small(gains[:, 2 * n + l, :], A[name][l].rearrange("(k p) -> p k", p=P))
                    small(lbr[:, l, :], A["lower_bounds"][l].rearrange("(k p) -> p k", p=P))
                    for j in range(3):
                        small(cw[:, l, j, :], A["conv_w"][l, j].rearrange("(k p) -> p k", p=P))
                    small(gn[:, l, :], A["hgrn_norm_w"][l:l + 1, :].to_broadcast([P, P]))
                    small(sg2[:, l, :], A["diff_subln_g_2"][l:l + 1, :].to_broadcast([P, P]))
                    small(lamr[:, l, :], A["diff_lambda_2"][l:l + 1].rearrange("a b c -> a (b c)").to_broadcast([P, 256]))
                small(posi[:], A["positions_2"].rearrange("o (h p) -> p (o h)", p=P))
                small(router[:], A["router_w"][0].rearrange("(k p) e -> p k e", p=P))
            assert count[0] == N_PARAMS
            first_layer(0)
            if stop > 1:
                first_layer(1)
            if stop > 2:
                row("final_norm", 4)
                second_layer(0)
            if stop > 3:
                second_layer(1)
                row("final_norm_g_2", 9)
            sp.wait_ge(S["x_ready"], {1: 2, 2: 4, 3: 7, 4: 10}[stop])
            sp.dma_start(out[0].rearrange("(h p) d -> p h d", p=P), x[:]).then_inc(S["out_done"], 16)
            sp.wait_ge(S["out_done"], 16)

        @block.tensor
        def _(pe):
            R = Ring()
            tiles = [0]

            def page(k, i, pages, dmas=1):
                p, before = R.at(k, i, pages)
                pe.wait_ge(landed[p], R.extra[p] + 16 * before + 16 * dmas)
                return p

            def norm_T(n):
                for h in range(TH):
                    pe.wait_ge(S["h_scaled"], 2 * n + h + 1)
                    for k in range(KD):
                        mm = pe.transpose(psXc[:, k, P * h:P * h + P], htok[:, h, P * k:P * k + P], ident[:])
                mm.then_inc(S["hT_psum"], 1)
                pe.wait_ge(S["hT_ready"], n + 1)

            def free_banks(index):
                if not (isinstance(index, int) and index < 2):
                    pe.wait_ge(S["tile_evac"], index - 1)

            def product(b, ks, i, pages, right, left, cols=W, per=4):
                ps = [page(k, i, pages) for k in ks]
                w = [ring[:, p, 0:per * cols].rearrange("p (a b) -> p a b", b=cols) for p in ps]
                n = per * len(ks)
                if right is not None:
                    for c in range(4):
                        for kk in range(n):
                            mm = pe.matmul(psG[:, b, c // 2, T * (c % 2):T * (c % 2) + T],
                                           w[kk // per][:, kk % per, P * c:P * c + P], right[:, kk, :],
                                           start=(kk == 0), stop=(kk == n - 1))
                else:
                    for h in range(TH):
                        for kk in range(n):
                            mm = pe.matmul(psG[:, b, h, 0:cols], left[:, kk, P * h:P * h + P], w[kk // per][:, kk % per, :],
                                           start=(kk == 0), stop=(kk == n - 1))
                return mm

            def run(count, turns=1, right=None, left=None, widths=None, per=4, pages_each=2):
                pages = pages_each * count
                base = tiles[0]

                def body(i):
                    for t in range(count):
                        free_banks(base + count * i + t)
                        product((base + t) % 2, range(pages_each * t, pages_each * t + pages_each), i, pages, right, left,
                                widths[t] if widths else W, per).then_inc(used, pages_each)
                if turns == 1:
                    body(0)
                else:
                    with pe.Fori(0, turns) as i:
                        body(i)
                tiles[0] += count * turns
                R.close(pages, turns)

            def residual(left):
                for t in range(2):
                    product(t, (2 * t, 2 * t + 1), 0, 4, None, left).then_inc(used, 2)
                R.close(4)

            def recurrence(l):
                pe.wait_ge(S["tile_evac"], tiles[0])
                pe.wait_ge(S["qa_on"], l + 1)
                for s in range(NSUB):
                    pe.wait_ge(S["ka_on"], NSUB * l + s + 1)
                    ka, qa = hc((bK, htok_f)[s % 2]), hc(bQ)
                    for n in range(HEADS * NC):
                        h, c = n // NC, n % NC
                        at = CH * (c % 2)
                        mm = pe.matmul(psXs[at:at + CH, 2 * h + c // 2, SUB * s:SUB * s + SUB], ka[:, n, :],
                                       qa[:, n, SUB * s:SUB * s + SUB], start=True, stop=True)
                    mm.then_inc(S["scores_on"], 1)
                pe.wait_ge(S["kl_on"], l + 1)
                klt = psGf.rearrange("p h (n d) -> p h n d", d=P)
                for h in range(HEADS):
                    for g in range(TH):
                        mm = pe.transpose(klt[:, g, h, :], hd(bK)[:, h, P * g:P * g + P], ident[:])
                mm.then_inc(S["klt_psum"], 1)
                pe.wait_ge(S["klt_sb"], l + 1)
                for c in range(NC - 1):
                    at, g = CH * (c % 2), c // 2
                    dst = psGf[:, c, :] if c < 2 else psX[:, 2:4, :].rearrange("p a b -> p (a b)")
                    for h in range(HEADS):
                        mm = pe.matmul(dst[:, P * h:P * h + P], htok[at:at + CH, g, P * h:P * h + P],
                                       zT[at:at + CH, g, P * h:P * h + P], start=True, stop=True)
                    mm.then_inc(S["u_on"], 1)
                pe.wait_ge(S["s_masked"], l + 1)
                pe.wait_ge(S["states_on"], 3 * (l + 1))
                pe.wait_ge(S["qe_on"], l + 1)
                for c in (0, 2, 1, 3):
                    at, g = CH * (c % 2), c // 2
                    for h in range(HEADS):
                        if c % 2 == 0:
                            dst = psG[0:CH, g, h // 4, P * (h % 4):P * (h % 4) + P]
                        else:
                            dst = psX[CH:P, 2 * g + h // 4, P * (h % 4):P * (h % 4) + P]
                        mm = pe.matmul(dst, sTm[at:at + CH, 2 * h + g, :], zT[at:at + CH, g, P * h:P * h + P],
                                       start=True, stop=(c == 0))
                        if c:
                            mm = pe.matmul(dst, hd(bF)[:, h, CH * c:CH * c + CH], states[c][:, h, :],
                                           start=False, stop=True)
                mm.then_inc(S["o_psum"], 1)
                pe.wait_ge(S["o_on"], l + 1)
                for h in range(HEADS):
                    for g in range(TH):
                        mm = pe.transpose(psXc[:, h, P * g:P * g + P], o_tok[:, g, P * h:P * h + P], ident[:])
                mm.then_inc(S["oT_psum"], 1)

            def feed_forward(n, turns):
                base = R.seq
                steps = n * STEPS

                def up(j, e):
                    last = steps + e * STEPS + (j - 1 if j == 0 else j - 2) + 1
                    if not (isinstance(last, int) and last <= 0):
                        pe.wait_ge(S["hid_on"], last)
                    for part in range(2):
                        p = page(ffn_page(j, part), e, PAGES_FFN)
                        w = ring[:, p, :].rearrange("p (a b) -> p a b", b=256)
                        for c in range(2):
                            for k in range(KD):
                                mm = pe.matmul(psG[:, j % 2, part, T * c:T * c + T], w[:, k, P * c:P * c + P], hT[:, k, :],
                                               start=(k == 0), stop=(k == KD - 1))
                    mm.then_inc(used, 2)

                def down(j, e):
                    if j == 0:
                        free = 2 * (n + e)
                        if not (isinstance(free, int) and free == 0):
                            pe.wait_ge(S["y_added"], free)
                    pe.wait_ge(S["hid_on"], steps + e * STEPS + j + 1)
                    p = page(ffn_page(j, 2), e, PAGES_FFN)
                    w = ring[:, p, :].rearrange("p (a b) -> p a b", b=D)
                    for h in range(TH):
                        for q in range(2):
                            for k in range(2):
                                mm = pe.matmul(psX[:, 2 * h + q, :], hid4[:, j % 2, k, P * h:P * h + P],
                                               w[:, k, W * q:W * q + W], start=(j == 0 and k == 0),
                                               stop=(j == STEPS - 1 and k == 1))
                    mm.then_inc(used, 1)

                def expert(e):
                    for j in range(STEPS):
                        up(j, e)
                        if j:
                            down(j - 1, e)
                    down(STEPS - 1, e)
                if turns == 1:
                    expert(0)
                else:
                    with pe.Fori(0, turns) as e:
                        expert(e)
                R.close(PAGES_FFN, turns)

            def first_layer(l):
                norm_T(2 * l)
                run(4, right=hT)
                run(4, left=hT)
                run(4, 2, right=hT)
                run(2, right=hT)
                recurrence(l)
                pe.wait_ge(S["oT_sb"], l + 1)
                pe.wait_ge(S["conv_ready"], l + 1)
                base = tiles[0]
                for t in range(4):
                    free_banks(base + t)
                    product((base + t) % 2, (2 * t, 2 * t + 1), 0, 8, oTv if t < 2 else w_u, None).then_inc(used, 2)
                tiles[0] += 4
                R.close(8)
                pe.wait_ge(S["merged"], l + 1)
                residual(w_q)
                norm_T(2 * l + 1)
                if l == 0:
                    feed_forward(0, 1)
                else:
                    for h in range(TH):
                        for k in range(KD):
                            mm = pe.matmul(psX[:, h, 0:EXPERTS], hT[:, k, P * h:P * h + P], router[:, k, :],
                                           start=(k == 0), stop=(k == KD - 1))
                    mm.then_inc(S["logits"], 1)
                    pe.wait_ge(S["lg_read"], 1)
                    feed_forward(1, EXPERTS)

            def scores(kind, qh, name):
                keys = P * (qh + 1)
                for p in range(2):
                    for c in range(4):
                        q, k = heads_of(kind, p, c)
                        at = 64 * p
                        mm = pe.matmul(psXc[:, 4 * p + c, 0:keys], QT[at:at + 64, q, P * qh:P * qh + P],
                                       QT[at:at + 64, k, 0:keys], start=True, stop=True)
                mm.then_inc(S[name], 1)

            def attend(kind, qh, a, n):
                pe.wait_ge(S["attn_out"], a)
                scores(kind, qh, "scores_full")
                pe.wait_ge(S["exp_on"], 8 * n + 8)
                for b in range(qh + 1):
                    for s in range(8):
                        mm = pe.transpose(psGf[:, b, P * s:P * s + P], sv[:, s, P * b:P * b + P], ident[:])
                mm.then_inc(S["pT_psum"], 1)
                pe.wait_ge(S["pT_act"], n + 1)
                if qh:
                    pe.wait_ge(S["pT_dve"], n // 8 * 4 + n % 4 + 1)
                wide = P if kind == "A" else 64
                o = psX[:].rearrange("p a b -> p (a b)")[:, 0:8 * wide].rearrange("p (s d) -> p s d", d=wide)
                for p in range(2):
                    for c in range(4):
                        col = {"A": A_V + P * c, "B": B_V, "S": C_VS + 64 * (c // 2), "W": C_VW + 64 * (c // 2)}[kind]
                        for b in range(qh + 1):
                            mm = pe.matmul(o[:, 4 * p + c, :], PT[:, b, 4 * p + c, :], zt[:, b, col:col + wide],
                                           start=(b == 0), stop=(b == qh))
                mm.then_inc(S["av_full"], 1)

            def compressed(qh, n, a):
                pe.wait_ge(S["attn_out"], a)
                for p in range(2):
                    for c in range(4):
                        at = 64 * p
                        mm = pe.matmul(psX[:, p, 16 * c:16 * c + NCMP], QT[at:at + 64, T_CQ + c, P * qh:P * qh + P],
                                       kcT[at:at + 64, c // 2, 0:NCMP], start=True, stop=True)
                mm.then_inc(S["cs_full"], 1)
                pe.wait_ge(S["cs_norm"], n + 1)
                for p in range(2):
                    mm = pe.transpose(psG[:, 0, 0, P * p:P * p + P], pcf[:, P * p:P * p + P], ident[:])
                mm.then_inc(S["pcT_psum"], 1)
                pe.wait_ge(S["pcT_sb"], n + 1)
                for c in range(4):
                    for p in range(2):
                        mm = pe.matmul(psX[:, c, 64 * p:64 * p + 64], pcT[32 * c:32 * c + 32, p, :],
                                       vcr[32 * c:32 * c + 32, c // 2, :], start=True, stop=True, tile_position=(32 * c, 0))
                mm.then_inc(S["cav_full"], 1)

            def compress(l):
                pe.wait_ge(S["cmp_in"], 16 * 7 * (l + 1))
                pe.transpose(psG[:, 0, 0, 0:64], pe_t[0:64, :], ident[0:64, 0:64]).then_inc(S["pe_psum"], 1)
                pe.wait_ge(S["cmp_x"], l + 1)
                ps = [page(k, 0, 4, 2) for k in range(4)]
                for n in range(2):
                    for g in range(2):
                        at = 64 * g
                        for r in range(32):
                            w = ring[at:at + 64, ps[2 * n + r // 16], :].rearrange("p (a b) -> p a b", b=P)
                            xs = cx[at:at + 64, 2 * n + r // 16, :].rearrange("p (m r) -> p m r", r=16)
                            mm = pe.matmul(psX[:, 2 * n + g, 0:NCMP], w[:, r % 16, :], xs[:, 0:NCMP, r % 16] if r < 16 else
                                           xs[:, 1:NCMP + 1, r % 16], start=(r == 0), stop=(r == 31))
                mm.then_inc(used, 4)
                R.close(4, 1, 2)
                pe.wait_ge(S["gelu_on"], l + 1)
                pe.wait_ge(S["hidc_on"], l + 1)
                for g in range(2):
                    pe.matmul(psG[:, 0, g, 0:NCMP], w2k, gel[:, g, 0:NCMP], start=True, stop=True)
                for g in range(2):
                    mm = pe.matmul(psG[:, 1, g, 0:64], hidc[:, g, :], w2v[:], start=True, stop=True)
                mm.then_inc(S["cmp_out"], 1)
                pe.wait_ge(S["cmp_sb"], 2 * (l + 1))

            def second_layer(l):
                norm_T(4 + 2 * l)
                run(4, 2, left=hT)
                run(3, left=hT, widths=[W, W, Z_COLS - 4096 - 2 * W])
                run(3, right=hT)
                run(3, right=hT)
                pe.wait_ge(S["rope_on"], l + 1)
                src = ([(zt, A_Q + P * c) for c in range(8)] + [(zt, B_Q + P * c) for c in range(4)]
                       + [(zt, I_Q + P * c) for c in range(4)] + [(zt, C_Q + P * c) for c in range(4)]
                       + [(crt, P * c) for c in range(4)] + [(kdf, P * c) for c in range(6)] + [(zt, C_KC), (zt, C_VC)])
                for g in range(8):
                    if g >= 2:
                        pe.wait_ge(S[("qT_act", "qT_dve")[g % 2]], 4 * l + g // 2)
                    for c in range(4):
                        t, col = src[4 * g + c]
                        for h in range(TH):
                            mm = pe.transpose(psXc[:, 4 * (g % 2) + c, P * h:P * h + P], t[:, h, col:col + P], ident[:])
                    mm.then_inc(S["qT_psum"], 1)
                pe.wait_ge(S["qT_act"], 4 * l + 4)
                pe.wait_ge(S["qT_dve"], 4 * l + 4)
                pe.wait_ge(S["tile_evac"], tiles[0])
                compress(l)
                a = ATT * l
                for qh in range(TH):
                    d = 2 * l + qh
                    pe.wait_ge(S["attn_out"], a)
                    scores("I", qh, "dots_full")
                    pe.wait_ge(S["relu_on"], d + 1)
                    attend("B", qh, a, 4 * d)
                    attend("A", qh, a + 1, 4 * d + 1)
                    compressed(qh, d, a + 2)
                    attend("S", qh, a + 3, 4 * d + 2)
                    attend("W", qh, a + 4, 4 * d + 3)
                    a += 5
                pe.wait_ge(S["branch_on"], l + 1)
                for b in range(3):
                    for c in range(4):
                        for h in range(TH):
                            dst = psXc[:, 4 * b + c, :] if b < 2 else psG4[:, c, :]
                            mm = pe.transpose(dst[:, P * h:P * h + P], zt[:, h, (A_G, B_G, C_G)[b] + P * c:
                                                                          (A_G, B_G, C_G)[b] + P * c + P], ident[:])
                mm.then_inc(S["bT_psum"], 1)
                pe.wait_ge(S["bT_act"], l + 1)
                pe.wait_ge(S["bT_dve"], l + 1)
                base = tiles[0]
                for b in range(3):
                    for t in range(2):
                        n = 2 * b + t
                        free_banks(base + n)
                        product((base + n) % 2, (n,), 0, 6, QT[:, 4 * b:4 * b + 4, :], None).then_inc(used, 1)
                tiles[0] += 6
                R.close(6)
                pe.wait_ge(S["up_merged"], l + 1)
                residual(QT[:, 12:20, :])
                pe.wait_ge(S["p_in"], 16 * (l + 1))
                pe.wait_ge(S["x_ready"], 6 + 2 * l)
                for k in range(2):
                    for h in range(TH):
                        mm = pe.transpose(psG[:, 0, 0, T * k + P * h:T * k + P * h + P], PL[:, h, P * k:P * k + P], ident[:])
                mm.then_inc(S["pT2_psum"], 1)
                pe.wait_ge(S["pT2_sb"], l + 1)
                p = page(0, 0, 1)
                w = ring[:, p, :].rearrange("p (a b) -> p a b", b=D)
                for t in range(2):
                    for h in range(TH):
                        for k in range(2):
                            mm = pe.matmul(psG[:, t, h, :], pTs[:, k, P * h:P * h + P], w[:, k, W * t:W * t + W],
                                           start=(k == 0), stop=(k == 1))
                mm.then_inc(used, 1)
                R.close(1)
                tiles[0] += 2
                norm_T(5 + 2 * l)
                run(2, left=hT)

            pe.wait_ge(S["consts"], N_CONSTS)
            pe.wait_ge(params, 16 * N_PARAMS)
            first_layer(0)
            if stop > 1:
                first_layer(1)
            if stop > 2:
                second_layer(0)
            if stop > 3:
                second_layer(1)

        @block.scalar
        def _(act):
            R = Ring()
            tiles = [0]

            def do(dst, src, func, name, **kw):
                act.activation(dst, src, func, **kw).then_inc(S[name], 1)

            def norm(m):
                act.wait_ge(S["x_ready"], m)
                for h in range(TH):
                    do(htok[:, h, :], x[:, h, :], ACT.Square, "squares", accum_out=st[:, h:h + 1])
                act.wait_ge(S["variance"], m + 1)
                do(st[:, 4:6], st[:, 2:4], ACT.Sqrt, "deviation")

            def read_out(count, turns, dst, per=2, func=ACT.Copy):
                base, seq = tiles[0], R.seq

                def body(i):
                    for t in range(count):
                        act.wait_ge(used, seq + per * (count * i + t + 1))
                        b = (base + t) % 2
                        d, s = dst(count * i + t, b)
                        act.activation(d, s, func).then_inc(S["tile_evac"], 1)
                if turns == 1:
                    body(0)
                else:
                    with act.Fori(0, turns) as i:
                        body(i)
                tiles[0] += count * turns
                R.close(per * count, turns)

            def feature(b):
                return psG[:, b].rearrange("p a (c t) -> p (a c) t", t=T)

            def recurrence(l):
                z_f = zF[:, 8:16, :]
                do(hd(bF), z_f, ACT.Sigmoid, "f_sig")
                do(z_f, z_f, ACT.Sigmoid, "z_sig", scale=-1.0)
                do(hd(bQ), w_q, ACT.Sigmoid, "q_sig")
                g = zT[:, :, 1024:2048]
                do(g, g, ACT.Silu, "silu_g")
                gates = zF[:, 40:56, :]
                do(gates, gates, ACT.Sigmoid, "gates_on")
                act.wait_ge(S["f_ready"], l + 1)
                do(bF, bF, ACT.Ln, "log_f")
                act.wait_ge(S["shifted_q"], l + 1)
                do(bQ, bQ, ACT.Exp, "exp_q")
                for s in range(NSUB):
                    act.wait_ge(S["shifted_k"], NSUB * l + s + 1)
                    v = hc((bK, htok_f)[s % 2])[:, :, 0:SUB * (s + 1)]
                    do(v, v, ACT.Exp, "exp_k")
                do(bF, bC, ACT.Exp, "exp_cum")
                do(eL, hc(bC)[:, :, CH - 1], ACT.Exp, "exp_last")
                act.wait_ge(S["shifted_l"], l + 1)
                do(bK, bK, ACT.Exp, "exp_l")
                act.wait_ge(S["klt_psum"], l + 1)
                do(htok_f, psG[:].rearrange("p a b c -> p (a b c)"), ACT.Copy, "klt_sb")
                act.wait_ge(S["o_psum"], l + 1)
                do(o_tok[0:CH], psGf[0:CH], ACT.Copy, "o_act")
                act.wait_ge(S["sub_var"], l + 1)
                do(hst[:], hst[:], ACT.Sqrt, "sub_dev")
                act.wait_ge(S["oT_psum"], l + 1)
                do(oTv, psXc, ACT.Copy, "oT_sb")

            def feed_forward(n, turns):
                seq, steps = R.seq, n * STEPS

                def expert(e):
                    for j in range(STEPS):
                        act.wait_ge(used, seq + e * PAGES_FFN + (2 if j == 0 else 3 * j + 1))
                        last = steps + e * STEPS + (j - 1 if j == 0 else j - 2) + 1
                        if not (isinstance(last, int) and last <= 0):
                            act.wait_ge(S["hid_on"], last)
                        act.activation(sil[:, j % 2, :], psG[:, j % 2, 0, :], ACT.Silu).then_inc(S["silu_on"], 1)
                if turns == 1:
                    expert(0)
                else:
                    with act.Fori(0, turns) as e:
                        expert(e)
                R.close(PAGES_FFN, turns)

            def first_layer(l):
                norm(2 * l)
                act.wait_ge(S["hT_ready"], 2 * l + 1)
                read_out(4, 1, lambda t, b: (zF[:, 4 * t:4 * t + 4, :], feature(b)))
                read_out(4, 1, lambda t, b: (zT[:, :, W * t:W * t + W], psG[:, b]))
                read_out(4, 2, lambda t, b: (zF[:, bass.ds(16 + 4 * t, 4), :], feature(b)))
                read_out(2, 1, lambda t, b: (zF[:, 48 + 4 * t:52 + 4 * t, :], feature(b)))
                act.wait_ge(S["tile_evac"], tiles[0])
                recurrence(l)
                read_out(4, 1, lambda t, b: (zF[:, 4 * t:4 * t + 4, :], feature(b)))
                R.close(4)
                norm(2 * l + 1)
                if l:
                    act.wait_ge(S["top_diff"], 1)
                    do(lg[:, 4, 0:2], lg[:, 3, 0:2], ACT.Exp, "top_exp")
                feed_forward(l, EXPERTS if l else 1)

            def softmax(n, keys):
                act.wait_ge(S["scores_cut"], n + 1)
                for s in range(8):
                    act.activation(sv[:, s, 0:keys], sv[:, s, 0:keys], ACT.Exp, bias=mx[:, s:s + 1], scale=SCALE,
                                   accum_out=den[:, s:s + 1]).then_inc(S["exp_on"], 1)
                act.wait_ge(S["pT_psum"], n + 1)
                do(PT[:, 0], psGf[:, 0, :].rearrange("p (s q) -> p s q", q=P), ACT.Copy, "pT_act")

            def second_layer(l):
                norm(5 + 2 * l)
                read_out(4, 2, lambda t, b: (zt[:, :, bass.ds(W * t, W)], psG[:, b]))
                read_out(3, 1, lambda t, b: (zt[:, :, 4096 + W * t:min(4096 + W * t + W, Z_COLS)],
                                             psG[:, b, :, 0:min(W, Z_COLS - 4096 - W * t)]))
                read_out(3, 1, lambda t, b: (zm[:, 4 * t:4 * t + 4, :], feature(b)), func=ACT.Sigmoid)
                read_out(3, 1, lambda t, b: (zm[:, 12 + 4 * t:16 + 4 * t, :], feature(b)), func=ACT.Sigmoid)
                for col in (A_G, B_G, C_G):
                    do(zt[:, :, col:col + W], zt[:, :, col:col + W], ACT.Silu, "branch_gates")
                do(bgs[:], zt[:, :, C_BG:C_BG + 24], ACT.Sigmoid, "branch_gates")
                for g in range(0, 8, 2):
                    act.wait_ge(S["qT_psum"], 8 * l + g + 1)
                    do(QT[:, 4 * g:4 * g + 4, :], psXc[:, 0:4, :], ACT.Copy, "qT_act")
                act.wait_ge(used, R.seq + 4)
                R.close(4, 1, 2)
                do(gel[:, :, 0:NCMP], psX[:, :, 0:NCMP], ACT.Gelu_apprx_tanh, "gelu_on")
                for qh in range(TH):
                    d, keys = 2 * l + qh, P * (qh + 1)
                    act.wait_ge(S["dots_full"], d + 1)
                    act.wait_ge(S["qT_dve"], 4 * l + 4)
                    if qh:
                        act.wait_ge(S["attn_out"], ATT * l + 5)
                    do(sv[:, :, 0:keys], psXc[:, :, 0:keys], ACT.Relu, "relu_on", scale=HD ** -0.5)
                    softmax(4 * d, keys)
                    softmax(4 * d + 1, keys)
                    act.wait_ge(S["sub2_var"], d + 1)
                    do(lg[:, 6, 0:4], lg[:, 5, 0:4], ACT.Sqrt, "sub2_dev")
                    act.wait_ge(S["cs_cut"], d + 1)
                    do(pc[:, :, 0:NCMP], pc[:, :, 0:NCMP], ACT.Exp, "cs_exp", scale=SCALE)
                    act.wait_ge(S["pcT_psum"], d + 1)
                    do(pcT[:], psG[:, 0, 0, 0:256].rearrange("p (a q) -> p a q", a=2), ACT.Copy, "pcT_sb")
                    softmax(4 * d + 2, keys)
                    softmax(4 * d + 3, keys)
                act.wait_ge(S["bT_psum"], l + 1)
                do(QT[:, 0:8, :], psXc, ACT.Copy, "bT_act")
                R.close(6)
                R.close(4)
                tiles[0] += 6
                act.wait_ge(S["x_ready"], 6 + 2 * l)
                act.dma_start(PL, A["p_2"][l, 0].rearrange("(h p) d -> p h d", p=P)).then_inc(S["p_in"], 16)
                act.wait_ge(S["pT2_psum"], l + 1)
                do(pTs, psG[:, 0, 0, :].rearrange("p (k t) -> p k t", k=2), ACT.Copy, "pT2_sb")
                act.wait_ge(used, R.seq + 1)
                R.close(1)
                for t in range(2):
                    do(pl[:, :, W * t:W * t + W], psG[:, t], ACT.Copy, "tile_evac")
                tiles[0] += 2
                norm(6 + 2 * l)
                read_out(2, 1, lambda t, b: (plg[:, :, W * t:W * t + W], psG[:, b]), func=ACT.Sigmoid)

            act.wait_ge(params, 16 * N_PARAMS)
            act.wait_ge(S["lb_max"], 1)
            do(lbt[:, 3:5, :], lbt[:, 1:3, :], ACT.Exp, "init_act")
            act.wait_ge(S["lam_sum"], 1)
            do(lams[:, 4:8], lams[:, 0:4], ACT.Exp, "init_act")
            act.wait_ge(S["angles"], 1)
            do(sinb[:], rr[:, 0:2, :], ACT.Sin, "init_act")
            do(cosb[:], rr[:, 2:4, :], ACT.Sin, "init_act")
            first_layer(0)
            if stop > 1:
                first_layer(1)
            if stop > 2:
                norm(4)
                second_layer(0)
            if stop > 3:
                second_layer(1)
                norm(9)

        @block.gpsimd
        def _(pool):
            n_of = {}

            def step(ins, name="pool_step"):
                ins.then_inc(S[name], 1)
                n_of[name] = n_of.get(name, 0) + 1
                pool.wait_ge(S[name], n_of[name])

            step(pool.memset(ones[:], 1.0))
            step(pool.memset(ident[:], 0.0))
            step(pool.affine_select(out=ident[:], in_=ident[:], compare_op=ALU.not_equal, fill=1.0, base=0,
                                    pattern=[[-1, P]], channel_multiplier=1), "consts")
            step(pool.memset(caus[:], 0.0))
            step(pool.affine_select(out=caus[:], in_=caus[:], compare_op=ALU.is_ge, fill=NEG, base=0,
                                    pattern=[[-1, P]], channel_multiplier=1), "consts")
            step(pool.memset(cm01[:], 1.0))
            step(pool.memset(cmask[:], 0.0))
            step(pool.affine_select(out=cm01[:], in_=cm01[:], compare_op=ALU.is_ge, fill=0.0, base=-31,
                                    pattern=[[P, TH], [-16, 16]], channel_multiplier=1), "consts")
            step(pool.affine_select(out=cmask[:], in_=cmask[:], compare_op=ALU.is_ge, fill=NEG, base=-31,
                                    pattern=[[P, TH], [-16, 16]], channel_multiplier=1), "consts")
            step(pool.memset(smask[:], 1))
            for at in (0, CH):
                step(pool.affine_select(out=smask[at:at + CH], in_=smask[at:at + CH], compare_op=ALU.is_ge, fill=0.0,
                                        base=0, pattern=[[1, CH]], channel_multiplier=-1), "consts")
            step(pool.memset(reset[:], 1.0))
            step(pool.memset(reset[:].rearrange("p (c t) -> p c t", t=CH)[:, :, 0:1], 0.0), "consts")
            step(pool.memset(sTm[:], 0.0), "consts")
            step(pool.memset(pc[:], 0.0))
            step(pool.memset(hidc[:], 0.0), "consts")

            for l in range(min(stop, 2)):
                pool.wait_ge(S["hT_ready"], 2 * l + 1)
                step(pool.memset(htok[:], 0.0))
                step(pool.memset(bK, 0.0), "ka_zero")
                pool.wait_ge(S["tile_evac"], 22 * l + 18)
                tmp = hT[:]

                def tap(j):
                    return bc(cw[:, l, j, :].unsqueeze(2), KD, T)

                pool.wait_ge(params, 16 * N_PARAMS)
                step(pool.tensor_tensor(w_b, w_b, w_u, ALU.mult))
                step(pool.tensor_tensor(w_u, w_b, tap(2), ALU.mult))
                for j, back in ((1, 1), (0, 2)):
                    step(pool.tensor_tensor(tmp, w_b, tap(j), ALU.mult))
                    step(pool.tensor_tensor(w_u[:, :, back:T], w_u[:, :, back:T], tmp[:, :, 0:T - back], ALU.add))
                step(pool.tensor_tensor(w_u, w_u, w_c, ALU.mult), "conv_ready")

        @block.vector
        def _(dve):
            R = Ring()
            n_of = {}
            tiles = [0]

            def go(ins, name="dve_step"):
                ins.then_inc(S[name], 1)
                n_of[name] = n_of.get(name, 0) + 1

            def own(name="dve_step"):
                dve.wait_ge(S[name], n_of[name])

            def step(ins, name="dve_step"):
                go(ins, name)
                own(name)

            def norm(m, n=None, gain=None):
                dve.wait_ge(S["squares"], 2 * m + 2)
                step(dve.tensor_scalar(st[:, 2:4], st[:, 0:2], 1.0 / D, EPS, ALU.mult, ALU.add), "variance")
                dve.wait_ge(S["deviation"], m + 1)
                step(dve.reciprocal(st[:, 6:8], st[:, 4:6]))
                if gain is None:
                    dve.wait_ge(S["row_in"], 16 * (1 if m == 4 else 2))
                    for h in range(TH):
                        step(dve.scalar_tensor_tensor(out=x[:, h, :], in0=x[:, h, :], scalar=st[:, 6 + h:7 + h], in1=frow,
                                                      op0=ALU.mult, op1=ALU.mult))
                    step(dve.tensor_copy(st[:, 8:9], st[:, 6:7]), "x_ready")
                    return
                for h in range(TH):
                    step(dve.tensor_scalar(htok[:, h, :], x[:, h, :], st[:, 6 + h:7 + h], None, ALU.mult), "h_scaled")
                dve.wait_ge(S["hT_psum"], n + 1)
                step(dve.tensor_tensor(hT[:], psXc, bc(gains[:, gain, :].unsqueeze(2), KD, T), ALU.mult), "hT_ready")

            def residual():
                for t in range(2):
                    dve.wait_ge(used, R.seq + 2 * t + 2)
                    step(dve.tensor_tensor(x[:, :, W * t:W * t + W], x[:, :, W * t:W * t + W], psG[:, t], ALU.add),
                         "x_ready" if t else "dve_step")
                R.close(4)

            def recurrence(l):
                dve.wait_ge(S["ka_zero"], l + 1)
                dve.wait_ge(S["q_sig"], l + 1)
                step(dve.scalar_tensor_tensor(out=w_q, in0=w_q, scalar=float(P) ** -0.5, in1=hd(bQ), op0=ALU.mult, op1=ALU.mult))
                step(dve.tensor_tensor(hd(bF), hd(bF), bc(oml[:, l, :].unsqueeze(2), HEADS, T), ALU.mult))
                step(dve.tensor_tensor(hd(bF), hd(bF), bc(lbT[:, l, :].unsqueeze(2), HEADS, T), ALU.add))
                step(dve.tensor_scalar(bF, bF, F_MIN, None, ALU.max), "f_ready")
                dve.wait_ge(S["z_sig"], l + 1)
                step(dve.tensor_tensor(w_k, w_k, bc(oml[:, l, :].unsqueeze(2), HEADS, T), ALU.mult))
                dve.wait_ge(S["log_f"], l + 1)
                for h in range(HEADS):
                    go(dve.tensor_tensor_scan(hd(bC)[:, h, :], reset[:], hd(bF)[:, h, :], 0.0, ALU.mult, ALU.add))
                own()
                cum = hc(bC)

                def anchor(s, width):
                    at = SUB * s + SUB // 2 - 1
                    return bc(cum[:, :, at:at + 1], HEADS * NC, width)

                sub = lambda b: b.rearrange("p (n r) -> p n r", r=SUB)
                step(dve.tensor_tensor(sub(bQ), sub(bC), bc(sub(bC)[:, :, SUB // 2 - 1:SUB // 2], T, SUB), ALU.subtract), "shifted_q")
                w_kc = w_k.rearrange("p h (c t) -> p (h c) t", t=CH)
                buf = [hc(bK), hc(htok_f)]

                def shift(s):
                    if s >= 2:
                        dve.wait_ge(S["scores_on"], NSUB * l + s - 1)
                    w = SUB * (s + 1)
                    go(dve.tensor_tensor(buf[s % 2][:, :, 0:w], anchor(s, w), cum[:, :, 0:w], ALU.subtract), "shifted_k")

                shift(0)
                dve.wait_ge(S["exp_q"], l + 1)
                step(dve.tensor_tensor(hd(bQ), hd(bQ), w_q, ALU.mult), "qa_on")
                for s in range(NSUB):
                    if s + 1 < NSUB:
                        shift(s + 1)
                    w = SUB * (s + 1)
                    dve.wait_ge(S["exp_k"], NSUB * l + s + 1)
                    step(dve.tensor_tensor(buf[s % 2][:, :, 0:w], buf[s % 2][:, :, 0:w], w_kc[:, :, 0:w], ALU.mult), "ka_on")
                dve.wait_ge(S["scores_on"], NSUB * l + 7)
                step(dve.tensor_tensor(hc(bK), bc(cum[:, :, CH - 1:CH], HEADS * NC, CH), cum, ALU.subtract), "shifted_l")
                dve.wait_ge(S["exp_cum"], l + 1)
                step(dve.tensor_tensor(hd(bF), hd(bF), w_q, ALU.mult), "qe_on")
                dve.wait_ge(S["exp_l"], l + 1)
                step(dve.tensor_tensor(hd(bK), hd(bK), w_k, ALU.mult), "kl_on")
                dve.wait_ge(S["scores_on"], NSUB * l + 8)
                step(dve.copy_predicated(sTm[:], bc(smask[:].unsqueeze(1), 16, CH), psXs), "s_masked")
                dve.wait_ge(S["exp_last"], l + 1)
                e4 = eL[:].rearrange("p (h c) -> p h c", c=NC)
                for c in range(3):
                    dve.wait_ge(S["u_on"], 3 * l + c + 1)
                    u = (psGf[:, c, :] if c < 2 else psX[:, 2:4, :].rearrange("p a b -> p (a b)")).rearrange(
                        "p (h d) -> p h d", d=P)
                    if c == 0:
                        step(dve.tensor_copy(states[1], u), "states_on")
                    else:
                        step(dve.tensor_tensor(states[c + 1], states[c], bc(e4[:, :, c:c + 1], HEADS, P), ALU.mult))
                        step(dve.tensor_tensor(states[c + 1], states[c + 1], u, ALU.add), "states_on")
                dve.wait_ge(S["o_psum"], l + 1)
                step(dve.tensor_copy(o_tok[CH:P], psX[CH:P].rearrange("p (h a) b -> p h (a b)", h=TH)), "o_dve")
                dve.wait_ge(S["o_act"], l + 1)
                o16 = bK.rearrange("p (n d) -> p n d", d=P)
                q16 = bQ.rearrange("p (n d) -> p n d", d=P)
                step(dve.tensor_tensor(bQ, bK, bK, ALU.mult))
                step(dve.tensor_reduce(hst[:], q16, AX_X, ALU.add))
                step(dve.tensor_scalar(hst[:], hst[:], 1.0 / P, EPS, ALU.mult, ALU.add), "sub_var")
                dve.wait_ge(S["sub_dev"], l + 1)
                step(dve.reciprocal(hst2[:], hst[:]))
                step(dve.tensor_tensor(o16, o16, bc(hst2[:].unsqueeze(2), 16, P), ALU.mult))
                step(dve.tensor_tensor(o16, o16, bc(gn[:, l, :].unsqueeze(1), 16, P), ALU.mult))
                dve.wait_ge(S["silu_g"], l + 1)
                step(dve.tensor_tensor(o_tok, o_tok, zT[:, :, 1024:2048], ALU.mult), "o_on")

            def feed_forward(n, turns, gated):
                seq, steps = R.seq, n * STEPS

                def expert(e):
                    for j in range(STEPS):
                        dve.wait_ge(S["silu_on"], steps + e * STEPS + j + 1)
                        if j >= 2:
                            dve.wait_ge(used, seq + e * PAGES_FFN + 3 * (j - 2) + 5)
                        elif j == 0:
                            dve.wait_ge(used, seq + e * PAGES_FFN)
                        dve.tensor_tensor(hid[:, j % 2, :], sil[:, j % 2, :], psG[:, j % 2, 1, :], ALU.mult).then_inc(S["hid_on"], 1)
                    dve.wait_ge(used, seq + (e + 1) * PAGES_FFN)
                    if not (isinstance(e, int) and e == 0):
                        dve.wait_ge(S["y_added"], 2 * (n + e))
                    for h in range(TH):
                        y = psX[:, 2 * h:2 * h + 2, :].rearrange("p a b -> p (a b)")
                        if gated:
                            ins = dve.scalar_tensor_tensor(out=x[:, h, :], in0=y, scalar=gate[:, h, bass.ds(e, 1)],
                                                           in1=x[:, h, :], op0=ALU.mult, op1=ALU.add)
                        else:
                            ins = dve.tensor_tensor(x[:, h, :], y, x[:, h, :], ALU.add)
                        ins.then_inc(S["y_added"], 1)
                if turns == 1:
                    expert(0)
                else:
                    with dve.Fori(0, turns) as e:
                        expert(e)
                dve.wait_ge(S["y_added"], 2 * (n + turns))
                step(dve.tensor_copy(st[:, 9:10], st[:, 6:7]), "x_ready")
                R.close(PAGES_FFN, turns)

            def route():
                dve.wait_ge(S["logits"], 1)
                L = lambda i: lg[:, i, :]
                for h in range(TH):
                    step(dve.tensor_copy(L(h), psX[:, h, 0:EXPERTS]), "dve_step")
                step(dve.tensor_copy(st[:, 10:11], st[:, 6:7]), "lg_read")
                for h in range(TH):
                    step(dve.max(out=L(7 + h), in_=L(h)))
                    step(dve.tensor_tensor(lg[:, 3, h:h + 1], lg[:, 7 + h, 1:2], lg[:, 7 + h, 0:1], ALU.subtract))
                step(dve.tensor_copy(st[:, 10:11], st[:, 6:7]), "top_diff")
                dve.wait_ge(S["top_exp"], 1)
                step(dve.tensor_scalar(lg[:, 4, 2:4], lg[:, 4, 0:2], 1.0, None, ALU.add))
                step(dve.reciprocal(lg[:, 4, 4:6], lg[:, 4, 2:4]))
                step(dve.tensor_tensor(lg[:, 4, 6:8], lg[:, 4, 4:6], lg[:, 4, 0:2], ALU.mult))
                for h in range(TH):
                    second = lg[:, 7 + h, 1:2]
                    step(dve.tensor_scalar(L(2), L(h), second, None, ALU.is_gt))
                    step(dve.tensor_reduce(lg[:, 9, 0:1], L(2), AX_X, ALU.add))
                    step(dve.tensor_scalar(L(5), L(h), second, None, ALU.is_equal))
                    step(dve.tensor_tensor_scan(L(6), ones[:, 0:EXPERTS], L(5), 0.0, ALU.mult, ALU.add))
                    step(dve.tensor_scalar(L(6), L(6), lg[:, 9, 0:1], 2.0, ALU.add, ALU.is_le))
                    step(dve.tensor_tensor(L(5), L(5), L(6), ALU.mult))
                    step(dve.tensor_scalar(L(2), L(2), lg[:, 4, 4 + h:5 + h], None, ALU.mult))
                    step(dve.scalar_tensor_tensor(out=gate[:, h, :], in0=L(5), scalar=lg[:, 4, 6 + h:7 + h], in1=L(2),
                                                  op0=ALU.mult, op1=ALU.add))

            def first_layer(l):
                norm(2 * l, 2 * l, 0 + l)
                R.close(8), R.close(8), R.close(8, 2), R.close(4)
                recurrence(l)
                base = tiles[0] = 22 * l
                dve.wait_ge(S["tile_evac"], base + 22)
                dve.wait_ge(S["gates_on"], l + 1)
                R.close(8)
                step(dve.tensor_tensor(w_q, w_q, zF[:, 40:48, :], ALU.mult))
                step(dve.tensor_tensor(w_k, w_k, zF[:, 48:56, :], ALU.mult))
                step(dve.tensor_tensor(w_q, w_q, w_k, ALU.add), "merged")
                residual()
                norm(2 * l + 1, 2 * l + 1, 2 + l)
                if l:
                    route()
                feed_forward(l, EXPERTS if l else 1, bool(l))

            def rope(v, heads):
                lo, hi = v[:, :, :, 0:ROT], v[:, :, :, ROT:2 * ROT]
                c = bc(cosb[:].unsqueeze(2), TH, heads, ROT)
                s = bc(sinb[:].unsqueeze(2), TH, heads, ROT)
                t = [rt[:, n, 0:TH * heads * ROT].rearrange("p (h n d) -> p h n d", h=TH, d=ROT) for n in range(4)]
                go(dve.tensor_tensor(t[0], lo, c, ALU.mult))
                go(dve.tensor_tensor(t[1], hi, s, ALU.mult))
                go(dve.tensor_tensor(t[2], hi, c, ALU.mult))
                go(dve.tensor_tensor(t[3], lo, s, ALU.mult))
                own()
                go(dve.tensor_tensor(lo, t[0], t[1], ALU.subtract))
                go(dve.tensor_tensor(hi, t[2], t[3], ALU.add))
                own()

            def by_head(t, col, heads):
                return t[:, :, col:col + 64 * heads].rearrange("p h (n d) -> p h n d", d=64)

            bg = lambda qh, n: bgs[:, qh, :].rearrange("p (c q r) -> p q c r", q=2, r=3)[:, :, :, n]
            slots = lambda v: v.rearrange("p (q c) -> p q c", q=2)
            by_slot = lambda v: v.rearrange("p (c q d) -> p q c d", q=2, d=64)
            flat = osum.rearrange("p s d -> p (s d)")

            def softmax_in(kind, qh, n):
                keys = P * (qh + 1)
                dve.wait_ge(S["scores_full"], n + 1)
                if kind == "B":
                    go(dve.tensor_tensor(sv[:, :, 0:keys], psXc[:, :, 0:keys], bc(bias[:, 0:keys].unsqueeze(1), 8, keys), ALU.add))
                else:
                    if qh:
                        go(dve.tensor_copy(sv[:, :, 0:P], psXc[:, :, 0:P]))
                    go(dve.tensor_tensor(sv[:, :, P * qh:keys], psXc[:, :, P * qh:keys], bc(caus[:].unsqueeze(1), 8, P), ALU.add))
                own()
                step(dve.tensor_reduce(mx[:], sv[:, :, 0:keys], AX_X, ALU.max))
                step(dve.tensor_scalar(mx[:], mx[:], -SCALE, None, ALU.mult), "scores_cut")

            def softmax_out(qh, n):
                dve.wait_ge(S["exp_on"], 8 * n + 8)
                step(dve.reciprocal(rden[:], den[:]))
                if qh:
                    dve.wait_ge(S["pT_psum"], n + 1)
                    step(dve.tensor_copy(PT[:, 1], psGf[:, 1, :].rearrange("p (s q) -> p s q", q=P)), "pT_dve")

            def index(l, qh, d):
                keys = P * (qh + 1)
                dve.wait_ge(S["relu_on"], d + 1)
                for s in range(8):
                    head = 2 * (s % 4) + s // 4
                    if s == 0:
                        step(dve.tensor_scalar(score[:, 0:keys], sv[:, s, 0:keys], iws[:, qh, head:head + 1], None, ALU.mult))
                    else:
                        step(dve.scalar_tensor_tensor(out=score[:, 0:keys], in0=sv[:, s, 0:keys], scalar=iws[:, qh, head:head + 1],
                                                      in1=score[:, 0:keys], op0=ALU.mult, op1=ALU.add))
                step(dve.tensor_tensor(score[:, P * qh:keys], score[:, P * qh:keys], caus[:], ALU.add))
                src = score
                for r in range(K_SEL // 8):
                    step(dve.max(out=m8[:], in_=src[:, 0:keys]))
                    step(dve.match_replace(out=(work, score)[r % 2][:, 0:keys], in_to_replace=m8[:], in_values=src[:, 0:keys],
                                           imm_value=TAKEN))
                    src = (work, score)[r % 2]
                step(dve.tensor_scalar(bias[:, 0:keys], src[:, 0:keys], TAKEN, 1.0, ALU.is_equal, ALU.subtract))
                step(dve.tensor_scalar(bias[:, 0:keys], bias[:, 0:keys], -NEG, None, ALU.mult))
                step(dve.tensor_tensor(bias[:, P * qh:keys], bias[:, P * qh:keys], caus[:], ALU.add))

            def attend(kind, l, qh, n):
                softmax_in(kind, qh, n)
                softmax_out(qh, n)
                dve.wait_ge(S["av_full"], n + 1)
                ps = psX[:].rearrange("p a b -> p (a b)")
                dve.wait_ge(S["branch_gates"], 4 * l + 4)
                if kind == "A":
                    step(dve.tensor_tensor(osum, ps[:, 0:1024].rearrange("p (s d) -> p s d", d=P), bc(rden[:].unsqueeze(2), 8, P), ALU.mult))
                    o, sq = osum[:, 0:4, :], osum[:, 4:8, :]
                    step(dve.scalar_tensor_tensor(out=o, in0=sq, scalar=nlam[:, l:l + 1], in1=o, op0=ALU.mult, op1=ALU.add))
                    step(dve.tensor_tensor(sq, o, o, ALU.mult))
                    step(dve.tensor_reduce(lg[:, 9, 0:4], sq, AX_X, ALU.add))
                    step(dve.tensor_scalar(lg[:, 5, 0:4], lg[:, 9, 0:4], 1.0 / P, EPS, ALU.mult, ALU.add), "sub2_var")
                    dve.wait_ge(S["sub2_dev"], 2 * l + qh + 1)
                    step(dve.reciprocal(lg[:, 7, 0:4], lg[:, 6, 0:4]))
                    step(dve.tensor_tensor(o, o, bc(lg[:, 7, 0:4].unsqueeze(2), 4, P), ALU.mult))
                    step(dve.tensor_tensor(o, o, bc(sg2[:, l, :].unsqueeze(1), 4, P), ALU.mult))
                    gated = zt[:, qh, A_G:A_G + W]
                    step(dve.tensor_tensor(gated, gated, flat[:, 0:W], ALU.mult), "attn_out")
                    return
                o = ps[:, 0:W].rearrange("p (q c d) -> p q c d", q=2, d=64)
                if kind != "B":
                    step(dve.tensor_tensor(slots(rden[:]), slots(rden[:]), bg(qh, 1 if kind == "S" else 2), ALU.mult))
                step(dve.tensor_tensor(by_slot(flat[:, 0:W]), o, bc(slots(rden[:]).unsqueeze(3), 2, 4, 64), ALU.mult))
                if kind == "B":
                    gated = zt[:, qh, B_G:B_G + W]
                    step(dve.tensor_tensor(gated, gated, flat[:, 0:W], ALU.mult), "attn_out")
                elif kind == "S":
                    step(dve.tensor_tensor(flat[:, W:2 * W], flat[:, W:2 * W], flat[:, 0:W], ALU.add), "attn_out")
                else:
                    step(dve.tensor_tensor(flat[:, W:2 * W], flat[:, W:2 * W], flat[:, 0:W], ALU.add))
                    gated = zt[:, qh, C_G:C_G + W]
                    step(dve.tensor_tensor(gated, gated, flat[:, W:2 * W], ALU.mult), "attn_out")

            def compressed(l, qh, d):
                dve.wait_ge(S["cs_full"], d + 1)
                v = pc[:, :, 0:NCMP]
                ps = psX[:, 0:2, 0:64].rearrange("p q (c n) -> p q c n", n=16)[:, :, :, 0:NCMP]
                v4 = v.rearrange("p (q c) n -> p q c n", q=2)
                cm = cmask[:, qh, 0:NCMP].unsqueeze(1).unsqueeze(1)
                step(dve.tensor_tensor(v4, ps, bc(cm, 2, 4, NCMP), ALU.add))
                step(dve.tensor_reduce(mx[:], v, AX_X, ALU.max))
                step(dve.tensor_tensor(v, v, bc(mx[:].unsqueeze(2), 8, NCMP), ALU.subtract), "cs_cut")
                dve.wait_ge(S["cs_exp"], d + 1)
                step(dve.tensor_reduce(den[:], v, AX_X, ALU.add))
                step(dve.reciprocal(rden[:], den[:]))
                step(dve.tensor_tensor(slots(rden[:]), slots(rden[:]), bg(qh, 0), ALU.mult))
                step(dve.tensor_tensor(v, v, bc(cm01[:, qh, 0:NCMP].unsqueeze(1), 8, NCMP), ALU.mult), "cs_norm")
                dve.wait_ge(S["cav_full"], d + 1)
                out4 = flat[:, W:2 * W].rearrange("p (c q d) -> p c q d", q=2, d=64)
                step(dve.tensor_tensor(out4, psX[:, :, 0:P].rearrange("p c (q d) -> p c q d", q=2),
                                       bc(slots(rden[:]).rearrange("p q c -> p c q").unsqueeze(3), 4, 2, 64), ALU.mult), "attn_out")

            def second_layer(l):
                base = tiles[0]
                norm(5 + 2 * l, 4 + 2 * l, 4 + l)
                R.close(8, 2), R.close(6)
                dve.wait_ge(S["tile_evac"], base + 11)
                step(dve.tensor_copy(crt, zt[:, :, C_Q:C_Q + W]))
                for t, col, heads in ((zt, A_Q, 16), (zt, B_Q, 9), (zt, I_Q, 9), (crt, 0, 8), (zt, C_KS, 2), (zt, C_KW, 2)):
                    rope(by_head(t, col, heads), heads)
                for w, col in enumerate((B_K, I_K, C_KS, C_KS + 64, C_KW, C_KW + 64)):
                    go(dve.tensor_copy(kdup[:, :, w, :].rearrange("p h (u d) -> p h u d", u=2),
                                       bc(zt[:, :, col:col + 64].unsqueeze(2), TH, 2, 64)))
                go(dve.tensor_scalar(iws[:], zt[:, :, I_W:I_W + 8], 8.0 ** -0.5, None, ALU.mult))
                own()
                step(dve.tensor_copy(st[:, 10:11], st[:, 6:7]), "rope_on")
                tiles[0] += 17
                R.close(6), R.close(6)
                for g in range(1, 8, 2):
                    dve.wait_ge(S["qT_psum"], 8 * l + g + 1)
                    step(dve.tensor_copy(QT[:, 4 * g:4 * g + 4, :], psXc[:, 4:8, :]), "qT_dve")
                dve.wait_ge(S["pe_psum"], l + 1)
                step(dve.tensor_copy(peT[:], psG[:, 0, 0, 0:64].rearrange("p (n r) -> p n r", n=2)))
                for n in range(2):
                    for a in range(2):
                        go(dve.tensor_tensor(cx[:, 2 * n + a, :].rearrange("p (m r) -> p m r", r=16),
                                             QT[:, T_KC + n, :].rearrange("p (m r) -> p m r", r=16),
                                             bc(peT[:, n, 16 * a:16 * a + 16].unsqueeze(1), 16, 16), ALU.add))
                own()
                step(dve.tensor_copy(st[:, 10:11], st[:, 6:7]), "cmp_x")
                R.close(4, 1, 2)
                dve.wait_ge(S["gelu_on"], l + 1)
                for g in range(2):
                    go(dve.tensor_copy(hidc[:, g, :].rearrange("p (j n) -> p j n", n=32)[:, :, 0:NCMP],
                                       bc(gel[:, 2 + g, 0:NCMP].unsqueeze(1), 4, NCMP)))
                own()
                step(dve.tensor_copy(st[:, 10:11], st[:, 6:7]), "hidc_on")
                dve.wait_ge(S["cmp_out"], l + 1)
                step(dve.tensor_copy(kcT[:, :, 0:NCMP], psG[:, 0, :, 0:NCMP]), "cmp_sb")
                step(dve.tensor_copy(vcr[:], psG[:, 1, :, 0:64]), "cmp_sb")
                for qh in range(TH):
                    d = 2 * l + qh
                    index(l, qh, d)
                    attend("B", l, qh, 4 * d)
                    attend("A", l, qh, 4 * d + 1)
                    compressed(l, qh, d)
                    attend("S", l, qh, 4 * d + 2)
                    attend("W", l, qh, 4 * d + 3)
                step(dve.tensor_copy(st[:, 10:11], st[:, 6:7]), "branch_on")
                dve.wait_ge(S["bT_psum"], l + 1)
                step(dve.tensor_copy(QT[:, 8:12, :], psG4), "bT_dve")
                for b in range(3):
                    for t in range(2):
                        n = 2 * b + t
                        dve.wait_ge(used, R.seq + n + 1)
                        ps = psG[:, tiles[0] % 2].rearrange("p a (c t) -> p (a c) t", t=T)
                        g = zm[:, 8 * b + 4 * t:8 * b + 4 * t + 4, :]
                        m = QT[:, 12 + 4 * t:16 + 4 * t, :]
                        if b == 0:
                            go(dve.tensor_tensor(m, ps, g, ALU.mult), "tile_evac")
                        else:
                            go(dve.tensor_tensor(g, ps, g, ALU.mult), "tile_evac")
                            dve.wait_ge(S["tile_evac"], l * 27 + TILES_1 + 17 + n + 1)
                            step(dve.tensor_tensor(m, m, g, ALU.add), "dve_step")
                        tiles[0] += 1
                R.close(6)
                step(dve.tensor_copy(st[:, 10:11], st[:, 6:7]), "up_merged")
                residual()
                R.close(1)
                norm(6 + 2 * l, 5 + 2 * l, 6 + l)
                R.close(4)
                tiles[0] += 4
                dve.wait_ge(S["tile_evac"], tiles[0])
                step(dve.tensor_tensor(pl, pl, plg, ALU.mult))
                step(dve.tensor_tensor(x[:], x[:], pl, ALU.add), "x_ready")

            dve.wait_ge(params, 16 * N_PARAMS)
            dve.wait_ge(S["consts"], N_CONSTS)
            B = lambda i: lbt[:, i, :]
            step(dve.tensor_tensor(B(0), lbr[:, 0, :], lbr[:, 1, :], ALU.max))
            go(dve.tensor_tensor(B(1), lbr[:, 0, :], B(0), ALU.subtract))
            go(dve.tensor_tensor(B(2), lbr[:, 1, :], B(0), ALU.subtract))
            own()
            step(dve.tensor_copy(st[:, 10:11], ones[:, 0:1]), "lb_max")
            for l in range(2):
                for n in range(2):
                    a = lamr[:, l, 128 * n:128 * n + 64]
                    step(dve.tensor_tensor(a, a, lamr[:, l, 128 * n + 64:128 * n + 128], ALU.mult))
                    step(dve.tensor_reduce(lams[:, 2 * l + n:2 * l + n + 1], a, AX_X, ALU.add))
            step(dve.tensor_copy(st[:, 10:11], ones[:, 0:1]), "lam_sum")
            step(dve.tensor_copy(posf[:], posi[:]))
            for j in range(ROT):
                go(dve.memset(inv[:, j:j + 1], float(np.float32(THETA) ** np.float32(-2.0 * j / (2 * ROT)))))
            own()
            for h in range(TH):
                step(dve.tensor_scalar(ang[:, h, :], inv[:], posf[:, h:h + 1], None, ALU.mult))
            for q in range(2):
                r, t = rr[:, 2 * q:2 * q + 2, :], tq[:]
                step(dve.tensor_scalar(t, ang[:], 1.0 / (2 * math.pi), 0.25 * q, ALU.mult, ALU.add))
                step(dve.tensor_scalar(t, t, ROUND, None, ALU.add))
                step(dve.tensor_scalar(t, t, -ROUND, None, ALU.add))
                step(dve.scalar_tensor_tensor(out=r, in0=t, scalar=-PI2[0], in1=ang[:], op0=ALU.mult, op1=ALU.add))
                for part in PI2[1:]:
                    step(dve.scalar_tensor_tensor(out=r, in0=t, scalar=-part, in1=r, op0=ALU.mult, op1=ALU.add))
                if q:
                    step(dve.tensor_scalar(r, r, math.pi / 2, None, ALU.add))
                step(dve.tensor_scalar(r, r, PI_UP, -PI_UP, ALU.min, ALU.max))
            step(dve.tensor_copy(st[:, 10:11], ones[:, 0:1]), "angles")
            dve.wait_ge(S["init_act"], 4)
            step(dve.tensor_tensor(B(0), B(3), B(4), ALU.add))
            step(dve.reciprocal(B(5), B(0)))
            go(dve.tensor_tensor(B(1), B(3), B(5), ALU.mult))
            go(dve.tensor_tensor(B(2), B(4), B(5), ALU.mult))
            own()
            step(dve.tensor_tensor(B(2), B(1), B(2), ALU.add))
            go(dve.tensor_tensor(lbT[:, 0, :], B(1), B(1), ALU.subtract))
            go(dve.tensor_tensor(lbT[:, 1, :], B(2), B(1), ALU.subtract))
            own()
            step(dve.tensor_scalar(oml[:], lbT[:], -1.0, 1.0, ALU.mult, ALU.add))
            for l in range(2):
                init = 0.8 - 0.6 * math.exp(-0.3 * l)
                step(dve.tensor_tensor(nlam[:, l:l + 1], lams[:, 5 + 2 * l:6 + 2 * l], lams[:, 4 + 2 * l:5 + 2 * l], ALU.subtract))
                step(dve.tensor_scalar(nlam[:, l:l + 1], nlam[:, l:l + 1], -init, None, ALU.add))
                step(dve.tensor_scalar(sg2[:, l, :], sg2[:, l, :], 1.0 - init, None, ALU.mult))
            first_layer(0)
            if stop > 1:
                first_layer(1)
            tiles[0] = TILES_1
            if stop > 2:
                norm(4)
                second_layer(0)
            if stop > 3:
                second_layer(1)
                norm(9)


_INS = ['x', 'w_in', 'lower_bounds', 'hgrn_norm_w', 'conv_w', 'w_proj_hgrn', 'w_proj_conv', 'w_out', 'norm_mix',
        'norm_ffn', 'dense_w1', 'dense_w3', 'dense_w2', 'router_w', 'expert_w1', 'expert_w3', 'expert_w2',
        'final_norm', 'p_2', 'positions_2', 'norm_g_2', 'w_in_2', 'diff_lambda_2', 'diff_subln_g_2', 'cmp_pe_k_2',
        'cmp_w1_k_2', 'cmp_w2_k_2', 'cmp_pe_v_2', 'cmp_w1_v_2', 'cmp_w2_v_2', 'w_up_2', 'w_out_2', 'ple_norm_g_2',
        'w_ple_2', 'w_ple_gate_2', 'final_norm_g_2']
_OUTS = [((1, T, D), 'float32')]
STOP = 4


def kernel(**inputs):
    import numpy as _np
    import concourse.bacc as _bacc
    from concourse import mybir as _mybir
    from concourse.bass_utils import run_bass_kernel_spmd as _run

    nc = _bacc.Bacc("TRN2", target_bir_lowering=False, num_devices=1, dynamic_dma_scratch_size=1024)
    arrays, args = {}, {}
    for name in _INS:
        a = _np.ascontiguousarray(inputs[name])
        arrays[f"in_{name}_dram"] = a
        args[name] = nc.dram_tensor(f"in_{name}_dram", a.shape, _mybir.dt.from_np(a.dtype), kind="ExternalInput").ap()
    outs = []
    for i, (shape, dtype) in enumerate(_OUTS):
        dt = _mybir.dt.from_np(_np.dtype(dtype))
        outs.append(nc.dram_tensor(f"out_{i}_dram", shape, dt, kind="ExternalOutput").ap())
    build(nc, args, *outs, stop=STOP)
    r = _run(nc, [arrays], core_ids=[0])
    got = tuple(r.results[0][f"out_{i}_dram"] for i in range(len(_OUTS)))
    return got[0]
```

```python
import math
from contextlib import ExitStack

import numpy as np

import concourse.bass as bass
from concourse import mybir

F32 = mybir.dt.float32
I32 = mybir.dt.int32
ALU = mybir.AluOpType
ACT = mybir.ActivationFunctionType
AX_X = mybir.AxisListType.X

P = 128
T = 256
TH = T // P
D = 1024
KD = D // P
W = 512
NP = 6
TOPS = 3
PAGE = 2048
EPS = 1e-6
NEG = -1e30
TAKEN = -3e38

HEADS = 8
CH = 64
NC = T // CH
SUB = 8
NSUB = CH // SUB
F_MIN = 1e-6
D_FF = 2816
STEPS = D_FF // 256
EXPERTS = 8

HD = 64
SCALE = HD ** -0.5
ROT = 8
THETA = 500000.0
K_SEL = 64
NCMP = 15
Z_COLS = 5600
A_Q, A_V, A_G = 0, 1024, 1536
B_Q, B_K, B_V, B_G = 2048, 2560, 2624, 2688
I_Q, I_K, I_W = 3200, 3712, 3776
C_Q, C_KC, C_VC, C_KS, C_VS, C_KW, C_VW = 3784, 4296, 4424, 4552, 4680, 4808, 4936
C_G, C_BG = 5064, 5576
T_AQ, T_AK, T_BQ, T_IQ, T_CQ, T_CR, T_BK, T_IK, T_KS, T_KW, T_KC, T_VC = 0, 4, 8, 12, 16, 20, 24, 25, 26, 28, 30, 31


N_PARAMS = 23
N_CONSTS = 9
TILES_1 = 44
ROUND = 1.5 * 2 ** 23
PI2 = (6.28125, 0.0019350051879882812, 3.019916e-7)
PI_UP = 3.1415925
ATT = 10
PAGES_FFN = 3 * STEPS

NAMES = """x_in params consts dve_step pool_step x_ready squares variance deviation h_scaled hT_psum hT_ready used
tile_evac f_sig z_sig q_sig f_ready log_f shifted_q exp_q qa_on ka_zero shifted_k exp_k ka_on scores_on
s_masked exp_cum exp_last shifted_l exp_l kl_on klt_psum klt_sb u_on states_on qe_on o_psum o_act o_dve silu_g
o_on oT_psum oT_sb conv_ready gates_on merged silu_on hid_on y_added logits top_diff top_exp row_in out_done
rope_on qT_psum qT_act qT_dve pe_psum cmp_in cmp_x gelu_on cmp_out cmp_sb dots_full relu_on scores_full
scores_cut exp_on pT_psum pT_act pT_dve av_full attn_out cs_full cs_cut cs_exp cs_norm pcT_psum pcT_sb
cav_full branch_gates branch_on bT_psum bT_act bT_dve up_merged p_in pT2_psum pT2_sb sub_var sub_dev init_act
angles hidc_on lg_read lam_sum lb_max sub2_var sub2_dev topped parted hT_topped hid_topped hT_parted
hid_parted""" 


def ffn_page(j, part):
    if part < 2:
        return part if j == 0 else 3 * j - 1 + part
    return 3 * j + 4 if j < STEPS - 1 else PAGES_FFN - 1


class Ring:

    def __init__(self):
        self.seq = 0
        self.parts = 0
        self.extra = [0] * NP

    def at(self, k, i, pages):
        n = self.seq + k
        return n % NP, n // NP + i * (pages // NP)

    def free(self, k, i, pages, places=NP):
        return self.seq + k + i * pages - places + 1

    def close(self, pages, turns=1, dmas=1, split=False):
        for k in range(pages if dmas > 1 else 0):
            self.extra[(self.seq + k) % NP] += 16 * (dmas - 1)
        self.seq += pages * turns
        self.parts += pages * turns if split else 0


def build(nc, A, out):
    ctx = ExitStack()
    with ctx:
        def sb(name, shape, dt=F32):
            return ctx.enter_context(nc.sbuf_tensor(name, shape, dt))[:]

        def sem(name):
            return ctx.enter_context(nc.semaphore(name))

        def sb_parts(name, shape, parts):
            with ExitStack() as overlay:
                views = [overlay.enter_context(nc.sbuf_tensor(n, s, mybir.dt.float32r))[:] for n, s in parts]
            return sb(name, shape), *views

        ring, ring_rest = sb_parts("ring", [P, NP, PAGE], [("ring_rest", [P, NP, PAGE])])
        tops = ctx.enter_context(nc.sbuf_tensor("tops", [P, TOPS, PAGE], mybir.dt.float32r))[:]
        x = sb("x_tok", [P, TH, D])
        hT, hT_rest = sb_parts("hT", [P, KD, T], [("hT_rest", [P, KD, T])])
        htok, hT_top = sb_parts("htok", [P, TH, D], [("hT_top", [P, KD, T])])
        AR, hid_top, hid_rest = sb_parts("arena", [P, 27136], [("hid_top", [P, 2, 2, T]), ("hid_rest", [P, 2, 2, T])])

        def area(at, *shape):
            n = 1
            for s in shape:
                n *= s
            v = AR[:, at:at + n]
            if len(shape) == 1:
                return v
            if len(shape) == 2:
                return v.rearrange("p (a b) -> p a b", b=shape[1])
            return v.rearrange("p (a b c) -> p a b c", b=shape[1], c=shape[2])

        zF = area(0, 56, T)
        zT = area(14336, TH, 2048)
        bF = area(18432, 2048)
        bC = area(20480, 2048)
        bQ = area(22528, 2048)
        bK = area(24576, 2048)
        sil = area(2048, 2, 512)
        hid = area(3072, 2, 512)
        zt = area(0, TH, Z_COLS)
        QT = area(11200, 32, T)
        zm = area(19392, 24, T)
        kdup = area(25536, TH, 6, P)
        osum = area(25536, 8, P)
        cx = area(26560, 2, T)
        crt = area(11200 + 28 * T, TH, W)
        sv = htok[:].rearrange("p h (s k) -> p (h s) k", k=T)
        PT = hT[:].rearrange("p (b s) (u q) -> p b (s u) q", b=2, u=2)
        PL = area(0, TH, T)
        pTs = area(512, 2, T)
        pl = area(1024, TH, D)
        plg = area(3072, TH, D)
        frow = area(6144, D)
        sTm = sb("scoresT", [P, 16, CH])
        sTf = sTm[:].rearrange("p s t -> p (s t)")
        score, work, bias = sTf[:, 0:T], sTf[:, T:2 * T], sTf[:, 2 * T:3 * T]
        pe_t, w2k = sTf[:, 3 * T:3 * T + P], sTf[:, 3 * T + P:4 * T]

        ident = sb("ident", [P, P])
        caus = sb("caus", [P, P])
        cmask = sb("cmask", [P, TH, 16])
        cm01 = sb("cm01", [P, TH, 16])
        smask = sb("smask", [P, CH], I32)
        ones = sb("ones", [P, T])
        reset = sb("reset", [P, T])
        gains = sb("gains", [P, 8, KD])
        lbr = sb("lbr", [P, 2, KD])
        lbt = sb("lbt", [P, 6, KD])
        lbT = sb("lbT", [P, 2, KD])
        oml = sb("oml", [P, 2, KD])
        cw = sb("cw", [P, 2, 3, KD])
        gn = sb("gn", [P, 2, P])
        sg2 = sb("sg2", [P, 2, P])
        lams = sb("lams", [P, 8])
        nlam = sb("nlam", [P, 2])
        posi = sb("posi", [P, TH], I32)
        posf = sb("posf", [P, TH])
        inv = sb("inv", [P, ROT])
        ang = sb("ang", [P, TH, ROT])
        rr = sb("rr", [P, 2 * TH, ROT])
        tq = sb("tq", [P, TH, ROT])
        cosb = sb("cosb", [P, TH, ROT])
        sinb = sb("sinb", [P, TH, ROT])
        rt = sb("rt", [P, 4, TH * 16 * ROT])
        lamr = rt[:, 0:2, :]
        router = sb("router", [P, KD, EXPERTS])
        st = sb("st", [P, 16])
        hst = sb("hst", [P, 16])
        hst2 = sb("hst2", [P, 16])
        eL = sb("eL", [P, 32])
        mx = sb("mx", [P, 8])
        den = sb("den", [P, 8])
        rden = sb("rden", [P, 8])
        m8 = sb("m8", [P, 8])
        iws = sb("iws", [P, TH, 8])
        bgs = sb("bgs", [P, TH, 24])
        peT = sb("peT", [P, 2, 32])
        gel = sb("gel", [P, 4, 16])
        hidc = sb("hidc", [P, 2, P])
        w2v = sb("w2v", [P, HD])
        kcT = sb("kcT", [P, 2, 16])
        vcr = sb("vcr", [P, 2, HD])
        pc = sb("pc", [P, 8, 32])
        pcT = sb("pcT", [P, 2, P])
        lg = sb("lg", [P, 10, 8])
        gate = sb("gate", [P, TH, 8])

        psG = ctx.enter_context(nc.psum_tensor("psG", [P, 2, 2, 512], F32))
        psX = ctx.enter_context(nc.psum_tensor("psX", [P, 4, 512], F32))

        landed = [sem(f"landed{p}") for p in range(NP)]
        S = {n: sem(n) for n in NAMES.split()}
        params, used = S["params"], S["used"]
        block = ctx.enter_context(nc.Block())

        def bc(ap, *shape):
            return ap.to_broadcast([ap.shape[0], *shape])

        def hc(b):
            return b.rearrange("p (h t) -> p h t", t=CH)

        def hd(b):
            return b.rearrange("p (h t) -> p h t", t=T)

        psGf = psG[:].rearrange("p a b c -> p a (b c)")
        psXc = psX[:].rearrange("p b (c t) -> p (b c) t", t=T)
        psXs = psX[:, 0:2, :].rearrange("p b (s t) -> p (b s) t", t=CH)
        psG4 = psG[:, 0, :, :].rearrange("p b (c t) -> p (b c) t", t=T)
        hTp = (hT_top, hT_rest)
        cmp_h = psG[:, 1, :, 0:32].rearrange("p g (n m) -> p n g m", m=16)
        cmp_k = psG[:, 1, 1, 32:64].rearrange("p (g m) -> p g m", m=16)
        cmp_v = psG[:, 1, 1, 64:192].rearrange("p (g d) -> p g d", d=64)

        def key_buffer(s):
            return hc((bK, bF)[s % 2])

        def part_of_page(pg, cols):
            return pg if cols == W else pg.rearrange("p (a b) -> p a b", b=W)[:, :, 0:cols]

        htok_f = htok[:].rearrange("p h d -> p (h d)")
        o_tok = bK.rearrange("p (h d) -> p h d", h=TH)
        states = [None] + [v.rearrange("p (h d) -> p h d", d=P) for v in (bC[:, 0:1024], bC[:, 1024:2048], htok_f[:, 0:1024])]
        kdf = kdup.rearrange("p h w d -> p h (w d)")
        pcf = pc[:].rearrange("p s n -> p (s n)")
        oTv = hd(bQ)
        w_q, w_k, w_b, w_c, w_u = (zF[:, 8 * n:8 * n + 8, :] for n in (0, 1, 2, 3, 4))

        def heads_of(kind, p, c):
            g = c // 2
            return {"A": (T_AQ + c, T_AK + c), "B": (T_BQ + c, T_BK), "I": (T_IQ + c, T_IK),
                    "S": (T_CR + c, T_KS + g), "W": (T_CR + c, T_KW + g), "C": (T_CQ + c, None)}[kind]

        @block.sync
        def _(sp):
            count = [0]

            def small(dst, src):
                sp.dma_start(dst, src).then_inc(params, 16)
                count[0] += 1

            R = Ring()

            def load(k, i, pages, src, cols, pitch=None):
                p, _ = R.at(k, i, pages)
                free = R.free(k, i, pages)
                if not (isinstance(free, int) and free <= 0):
                    sp.wait_ge(used, free)
                dst = ring[:, p, :].rearrange("p (a b) -> p a b", b=pitch or cols)
                sp.dma_start(dst[:, 0:src.shape[1], 0:cols], src).then_inc(landed[p], 16)

            def rows(w):
                return w.rearrange("(k p) n -> p k n", p=P)

            def project(k, i, pages, w, col, cols=W):
                for h in range(2):
                    load(k + h, i, pages, rows(w)[:, 4 * h:4 * h + 4, bass.ds(col, cols)], cols, W)

            def ffn(w1, w3, w2, i=0, m=0, pages=PAGES_FFN):
                at = m * PAGES_FFN
                for j in range(STEPS + 1):
                    if j < STEPS:
                        load(at + ffn_page(j, 0), i, pages, w1[:, :, 256 * j:256 * j + 256], 256)
                        load(at + ffn_page(j, 1), i, pages, w3[:, :, 256 * j:256 * j + 256], 256)
                    if j:
                        load(at + ffn_page(j - 1, 2), i, pages, w2[:, 2 * j - 2:2 * j, :], D)

            def small_loads():
                for l in range(2):
                    for n, name in enumerate(("norm_mix", "norm_ffn", "norm_g_2", "ple_norm_g_2")):
                        if n or l:
                            small(gains[:, 2 * n + l, :], A[name][l].rearrange("(k p) -> p k", p=P))
                    small(lbr[:, l, :], A["lower_bounds"][l].rearrange("(k p) -> p k", p=P))
                    for j in range(3):
                        small(cw[:, l, j, :], A["conv_w"][l, j].rearrange("(k p) -> p k", p=P))
                    small(gn[:, l, :], A["hgrn_norm_w"][l:l + 1, :].to_broadcast([P, P]))
                    small(sg2[:, l, :], A["diff_subln_g_2"][l:l + 1, :].to_broadcast([P, P]))
                    small(lamr[:, l, :], A["diff_lambda_2"][l:l + 1].rearrange("a b c -> a (b c)").to_broadcast([P, 256]))
                small(posi[:], A["positions_2"].rearrange("o (h p) -> p (o h)", p=P))
                small(router[:], A["router_w"][0].rearrange("(k p) e -> p k e", p=P))
                assert count[0] == N_PARAMS

            def first_layer(l):
                w = A["w_in"][l]
                for t in range(18):
                    project(2 * t, 0, 36, w, W * t)
                    if l == 0 and t == 2:
                        with nc.allow_non_contiguous_dma(reason="gains by feature, a few thousand elements once"):
                            small_loads()
                R.close(36)
                for t in range(2):
                    project(2 * t, 0, 8, A["w_proj_hgrn"][l], W * t)
                for t in range(2):
                    project(2 * t + 4, 0, 8, A["w_proj_conv"][l], W * t)
                R.close(8)
                for t in range(2):
                    project(2 * t, 0, 4, A["w_out"][l], W * t)
                R.close(4)
                if l == 0:
                    ffn(rows(A["dense_w1"][0]), rows(A["dense_w3"][0]), rows(A["dense_w2"][0]))
                    R.close(PAGES_FFN)
                else:
                    with sp.Fori(0, EXPERTS // 2) as i:
                        for m in range(2):
                            ffn(*[A[w][0, bass.ds(2 * i + m, 1)].rearrange("o (k p) n -> p (o k) n", p=P)
                                  for w in ("expert_w1", "expert_w3", "expert_w2")], i, m, 2 * PAGES_FFN)
                    R.close(2 * PAGES_FFN, EXPERTS // 2)

            def second_layer(l):
                w = A["w_in_2"][l]
                for t in range(11):
                    project(2 * t, 0, 22, w, W * t, min(W, Z_COLS - W * t))
                R.close(22)
                for t in range(6):
                    project(2 * t, 0, 12, w, Z_COLS + W * t)
                R.close(12)
                if l:
                    sp.wait_ge(S["cmp_sb"], 2 * l)
                for g in range(2):
                    sp.dma_start(w2k[:, 64 * g:64 * g + 64], A["cmp_w2_k_2"][l]).then_inc(S["cmp_in"], 16)
                    sp.dma_start(pe_t[0:32, 64 * g:64 * g + 64], A["cmp_pe_k_2"][l]).then_inc(S["cmp_in"], 16)
                    sp.dma_start(pe_t[32:64, 64 * g:64 * g + 64], A["cmp_pe_v_2"][l]).then_inc(S["cmp_in"], 16)
                sp.dma_start(w2v[:], A["cmp_w2_v_2"][l]).then_inc(S["cmp_in"], 16)
                for n, name in enumerate(("cmp_w1_k_2", "cmp_w1_v_2")):
                    for h in range(2):
                        p, _ = R.at(2 * n + h, 0, 4)
                        sp.wait_ge(used, R.free(2 * n + h, 0, 4))
                        for g in range(2):
                            sp.dma_start(ring[64 * g:64 * g + 64, p, :].rearrange("p (a b) -> p a b", b=P),
                                         A[name][l, 16 * h:16 * h + 16].rearrange("l d f -> d l f")).then_inc(landed[p], 16)
                R.close(4, 1, 2)
                for b in range(3):
                    for t in range(2):
                        load(2 * b + t, 0, 6, rows(A["w_up_2"][l, b])[:, :, W * t:W * t + W], W)
                R.close(6)
                for t in range(2):
                    project(2 * t, 0, 4, A["w_out_2"][l], W * t)
                R.close(4)
                load(0, 0, 1, rows(A["w_ple_2"][l]), D)
                R.close(1)
                for t in range(2):
                    project(2 * t, 0, 4, A["w_ple_gate_2"][l], W * t)
                R.close(4)

            with nc.allow_non_contiguous_dma(reason="gains by feature, a few thousand elements once"):
                sp.dma_start(x[:], A["x"][0].rearrange("(h p) d -> p h d", p=P)).then_inc(S["x_in"], 16)
                sp.dma_start(gains[:, 0, :], A["norm_mix"][0].rearrange("(k p) -> p k", p=P)).then_inc(S["x_in"], 16)
            first_layer(0)
            first_layer(1)
            second_layer(0)
            second_layer(1)
            sp.wait_ge(S["x_ready"], 10)
            sp.dma_start(out[0].rearrange("(h p) d -> p h d", p=P), x[:]).then_inc(S["out_done"], 16)
            sp.wait_ge(S["out_done"], 16)

        @block.tensor
        def _(pe):
            R = Ring()
            tiles = [0]

            def page(k, i, pages, dmas=1):
                p, before = R.at(k, i, pages)
                pe.wait_ge(landed[p], R.extra[p] + 16 * before + 16 * dmas)
                return p

            def norm_T(n):
                for h in range(TH):
                    pe.wait_ge(S["h_scaled"], 2 * n + h + 1)
                    for k in range(KD):
                        mm = pe.transpose(psXc[:, k, P * h:P * h + P], htok[:, h, P * k:P * k + P], ident[:])
                mm.then_inc(S["hT_psum"], 1)
                pe.wait_ge(S["hT_ready"], 2 * n + 2)

            def free_banks(index):
                if not (isinstance(index, int) and index < 2):
                    pe.wait_ge(S["tile_evac"], index - 1)

            def three(dst, left, right, start, stop):
                for n, (a, c) in enumerate(((0, 0), (0, 1), (1, 0))):
                    mm = pe.matmul(dst, left[a], right[c], start=start and n == 0, stop=stop and n == 2)
                return mm

            def both(k, i, pages, cols):
                pe.wait_ge(S["parted"], R.parts + k + i * pages + 1)
                n = R.seq + k
                return [v.rearrange("p (a b) -> p a b", b=cols) for v in (tops[:, n % TOPS, :], ring_rest[:, n % NP, :])]

            def product_of_parts(b, ks, i, pages, feature_major, cols):
                for n, k in enumerate(ks):
                    w = both(k, i, pages, W)
                    for c in range(4 if feature_major else TH):
                        for kk in range(4):
                            at = 4 * n + kk
                            if feature_major:
                                mm = three(psG[:, b, c // 2, T * (c % 2):T * (c % 2) + T],
                                           [v[:, kk, P * c:P * c + P] for v in w], [v[:, at, :] for v in hTp],
                                           at == 0 and c % 2 == 0, at == KD - 1 and c % 2 == 1)
                            else:
                                mm = three(psG[:, b, c, 0:cols], [v[:, at, P * c:P * c + P] for v in hTp],
                                           [v[:, kk, 0:cols] for v in w], at == 0, at == KD - 1)
                    mm.then_inc(used, 1)

            def product(b, ks, i, pages, right, left, cols=W, per=4):
                ps = [page(k, i, pages) for k in ks]
                w = [ring[:, p, 0:per * cols].rearrange("p (a b) -> p a b", b=cols) for p in ps]
                n = per * len(ks)
                if right is not None:
                    for c in range(4):
                        for kk in range(n):
                            mm = pe.matmul(psG[:, b, c // 2, T * (c % 2):T * (c % 2) + T],
                                           w[kk // per][:, kk % per, P * c:P * c + P], right[:, kk, :],
                                           start=(kk == 0), stop=(kk == n - 1))
                else:
                    for h in range(TH):
                        for kk in range(n):
                            mm = pe.matmul(psG[:, b, h, 0:cols], left[:, kk, P * h:P * h + P], w[kk // per][:, kk % per, :],
                                           start=(kk == 0), stop=(kk == n - 1))
                return mm

            def run_parts(count, feature_major, widths=None, after=None):
                for t in range(count):
                    free_banks(tiles[0] + t)
                    product_of_parts((tiles[0] + t) % 2, (2 * t, 2 * t + 1), 0, 2 * count, feature_major,
                                     widths[t] if widths else W)
                    if after:
                        after(t)
                tiles[0] += count
                R.close(2 * count, split=True)

            def residual(left):
                for t in range(2):
                    product(t, (2 * t, 2 * t + 1), 0, 4, None, left).then_inc(used, 2)
                R.close(4)

            def anchored_scores(l, pair):
                if pair == 0:
                    pe.wait_ge(S["qa_on"], l + 1)
                for s in (2 * pair, 2 * pair + 1):
                    pe.wait_ge(S["ka_on"], NSUB * l + s + 1)
                    ka, qa = key_buffer(s), hc(bQ)
                    for n in range(HEADS * NC):
                        h, c = n // NC, n % NC
                        at = CH * (c % 2)
                        mm = pe.matmul(psXs[at:at + CH, 2 * h + c // 2, SUB * s:SUB * s + SUB], ka[:, n, :],
                                       qa[:, n, SUB * s:SUB * s + SUB], start=True, stop=True)
                    mm.then_inc(S["scores_on"], 1)

            def recurrence(l):
                pe.wait_ge(S["tile_evac"], tiles[0])
                pe.wait_ge(S["kl_on"], l + 1)
                klt = psGf.rearrange("p h (n d) -> p h n d", d=P)
                for h in range(HEADS):
                    for g in range(TH):
                        mm = pe.transpose(klt[:, g, h, :], hd(bK)[:, h, P * g:P * g + P], ident[:])
                mm.then_inc(S["klt_psum"], 1)
                pe.wait_ge(S["klt_sb"], l + 1)
                for c in range(NC - 1):
                    at, g = CH * (c % 2), c // 2
                    dst = psGf[:, c, :] if c < 2 else psX[:, 2:4, :].rearrange("p a b -> p (a b)")
                    for h in range(HEADS):
                        mm = pe.matmul(dst[:, P * h:P * h + P], htok[at:at + CH, g, P * h:P * h + P],
                                       zT[at:at + CH, g, P * h:P * h + P], start=True, stop=True)
                    mm.then_inc(S["u_on"], 1)
                pe.wait_ge(S["s_masked"], l + 1)
                pe.wait_ge(S["states_on"], 3 * (l + 1))
                pe.wait_ge(S["qe_on"], l + 1)
                for c in (0, 2, 1, 3):
                    at, g = CH * (c % 2), c // 2
                    for h in range(HEADS):
                        if c % 2 == 0:
                            dst = psG[0:CH, g, h // 4, P * (h % 4):P * (h % 4) + P]
                        else:
                            dst = psX[CH:P, 2 * g + h // 4, P * (h % 4):P * (h % 4) + P]
                        mm = pe.matmul(dst, sTm[at:at + CH, 2 * h + g, :], zT[at:at + CH, g, P * h:P * h + P],
                                       start=True, stop=(c == 0))
                        if c:
                            mm = pe.matmul(dst, hd(bF)[:, h, CH * c:CH * c + CH], states[c][:, h, :],
                                           start=False, stop=True)
                mm.then_inc(S["o_psum"], 1)
                pe.wait_ge(S["o_on"], l + 1)
                for h in range(HEADS):
                    for g in range(TH):
                        mm = pe.transpose(psXc[:, h, P * g:P * g + P], o_tok[:, g, P * h:P * h + P], ident[:])
                mm.then_inc(S["oT_psum"], 1)

            def feed_forward(n, turns, each):
                pages = each * PAGES_FFN

                def up(j, e, m):
                    at, steps = m * PAGES_FFN, (n + m) * STEPS
                    last = steps + e * each * STEPS + (j - 1 if j == 0 else j - 2) + 1
                    if not (isinstance(last, int) and last <= 0):
                        pe.wait_ge(S["hid_on"], last)
                    for part in range(2):
                        w = both(ffn_page(j, part) + at, e, pages, 256)
                        for c in range(2):
                            for k in range(KD):
                                mm = three(psG[:, j % 2, part, T * c:T * c + T], [v[:, k, P * c:P * c + P] for v in w],
                                           [v[:, k, :] for v in hTp], k == 0, k == KD - 1)
                        mm.then_inc(used, 1)

                def down(j, e, m):
                    at, steps = m * PAGES_FFN, (n + m) * STEPS
                    if j == 0:
                        free = 2 * (n + m + e * each)
                        if not (isinstance(free, int) and free == 0):
                            pe.wait_ge(S["y_added"], free)
                    w = both(ffn_page(j, 2) + at, e, pages, D)
                    pe.wait_ge(S["hid_parted"], steps + e * each * STEPS + j + 1)
                    for h in range(TH):
                        for q in range(2):
                            for k in range(2):
                                mm = three(psX[:, 2 * h + q, :], [v[:, j % 2, k, P * h:P * h + P] for v in (hid_top, hid_rest)],
                                           [v[:, k, W * q:W * q + W] for v in w], j == 0 and k == 0,
                                           j == STEPS - 1 and k == 1)
                    mm.then_inc(used, 1)

                def expert(e, m):
                    for j in range(STEPS):
                        up(j, e, m)
                        if j:
                            down(j - 1, e, m)
                    down(STEPS - 1, e, m)
                if turns == 1:
                    expert(0, 0)
                else:
                    with pe.Fori(0, turns) as e:
                        for m in range(each):
                            expert(e, m)
                R.close(pages, turns, split=True)

            def first_layer(l):
                norm_T(2 * l)
                pe.wait_ge(S["hT_parted"], 4 * l + 2)
                run_parts(4, True)
                run_parts(4, False)
                run_parts(10, True, after=lambda t: anchored_scores(l, t // 3) if t in (2, 5, 8) else None)
                anchored_scores(l, 3)
                recurrence(l)
                pe.wait_ge(S["oT_sb"], l + 1)
                pe.wait_ge(S["conv_ready"], l + 1)
                base = tiles[0]
                for t in range(4):
                    free_banks(base + t)
                    product((base + t) % 2, (2 * t, 2 * t + 1), 0, 8, oTv if t < 2 else w_u, None).then_inc(used, 2)
                tiles[0] += 4
                R.close(8)
                pe.wait_ge(S["merged"], l + 1)
                residual(w_q)
                norm_T(2 * l + 1)
                if l == 0:
                    pe.wait_ge(S["hT_parted"], 4)
                    feed_forward(0, 1, 1)
                else:
                    pe.wait_ge(params, 16 * N_PARAMS)
                    for h in range(TH):
                        for k in range(KD):
                            mm = pe.matmul(psX[:, h, 0:EXPERTS], hT[:, k, P * h:P * h + P], router[:, k, :],
                                           start=(k == 0), stop=(k == KD - 1))
                    mm.then_inc(S["logits"], 1)
                    pe.wait_ge(S["lg_read"], 1)
                    pe.wait_ge(S["hT_parted"], 8)
                    feed_forward(1, EXPERTS // 2, 2)

            def scores(kind, qh, name):
                keys = P * (qh + 1)
                for p in range(2):
                    for c in range(4):
                        q, k = heads_of(kind, p, c)
                        at = 64 * p
                        mm = pe.matmul(psXc[:, 4 * p + c, 0:keys], QT[at:at + 64, q, P * qh:P * qh + P],
                                       QT[at:at + 64, k, 0:keys], start=True, stop=True)
                mm.then_inc(S[name], 1)

            def attend(kind, qh, a, n, meanwhile=None):
                pe.wait_ge(S["attn_out"], a)
                scores(kind, qh, "scores_full")
                if meanwhile:
                    meanwhile()
                pe.wait_ge(S["exp_on"], 8 * n + 8)
                for b in range(qh + 1):
                    for s in range(8):
                        mm = pe.transpose(psGf[:, b, P * s:P * s + P], sv[:, s, P * b:P * b + P], ident[:])
                mm.then_inc(S["pT_psum"], 1)
                pe.wait_ge(S["pT_act"], n + 1)
                if qh:
                    pe.wait_ge(S["pT_dve"], n // 8 * 4 + n % 4 + 1)
                wide = P if kind == "A" else 64
                o = psX[:].rearrange("p a b -> p (a b)")[:, 0:8 * wide].rearrange("p (s d) -> p s d", d=wide)
                for p in range(2):
                    for c in range(4):
                        col = {"A": A_V + P * c, "B": B_V, "S": C_VS + 64 * (c // 2), "W": C_VW + 64 * (c // 2)}[kind]
                        for b in range(qh + 1):
                            mm = pe.matmul(o[:, 4 * p + c, :], PT[:, b, 4 * p + c, :], zt[:, b, col:col + wide],
                                           start=(b == 0), stop=(b == qh))
                mm.then_inc(S["av_full"], 1)

            def compressed(qh, n, a):
                pe.wait_ge(S["attn_out"], a)
                for p in range(2):
                    for c in range(4):
                        at = 64 * p
                        mm = pe.matmul(psX[:, p, 16 * c:16 * c + NCMP], QT[at:at + 64, T_CQ + c, P * qh:P * qh + P],
                                       kcT[at:at + 64, c // 2, 0:NCMP], start=True, stop=True)
                mm.then_inc(S["cs_full"], 1)
                pe.wait_ge(S["cs_norm"], n + 1)
                for p in range(2):
                    mm = pe.transpose(psG[:, 0, 0, P * p:P * p + P], pcf[:, P * p:P * p + P], ident[:])
                mm.then_inc(S["pcT_psum"], 1)
                pe.wait_ge(S["pcT_sb"], n + 1)
                for c in range(4):
                    for p in range(2):
                        mm = pe.matmul(psX[:, c, 64 * p:64 * p + 64], pcT[32 * c:32 * c + 32, p, :],
                                       vcr[32 * c:32 * c + 32, c // 2, :], start=True, stop=True, tile_position=(32 * c, 0))
                mm.then_inc(S["cav_full"], 1)

            def compress(l, n, halves):
                pe.wait_ge(S["cmp_x"], l + 1)
                for half in halves:
                    p = page(2 * n + half, 0, 4, 2)
                    for r in range(16):
                        for g in range(2):
                            at = 64 * g
                            w = ring[at:at + 64, p, :].rearrange("p (a b) -> p a b", b=P)
                            xs = (cx[:, n, :] if half else QT[:, T_KC + n, :]).rearrange("p (m r) -> p m r", r=16)
                            mm = pe.matmul(cmp_h[:, n, g, 0:NCMP], w[:, r, :], xs[at:at + 64, half:NCMP + half, r],
                                           start=(half == 0 and r == 0), stop=(half == 1 and r == 15))
                    mm.then_inc(used, 1)

            def compress_out(l):
                pe.wait_ge(S["gelu_on"], l + 1)
                pe.wait_ge(S["hidc_on"], l + 1)
                for g in range(2):
                    pe.matmul(cmp_k[:, g, 0:NCMP], w2k, gel[:, g, 0:NCMP], start=True, stop=True)
                for g in range(2):
                    mm = pe.matmul(cmp_v[:, g, :], hidc[:, g, :], w2v[:], start=True, stop=True)
                mm.then_inc(S["cmp_out"], 1)
                pe.wait_ge(S["cmp_sb"], 2 * (l + 1))

            def second_layer(l):
                norm_T(4 + 2 * l)
                pe.wait_ge(S["hT_parted"], 2 * (5 + 2 * l))
                run_parts(11, False, [min(W, Z_COLS - W * t) for t in range(11)])
                run_parts(6, True)
                pe.wait_ge(S["rope_on"], l + 1)
                src = ([(zt, A_Q + P * c) for c in range(8)] + [(zt, B_Q + P * c) for c in range(4)]
                       + [(zt, I_Q + P * c) for c in range(4)] + [(zt, C_Q + P * c) for c in range(4)]
                       + [(crt, P * c) for c in range(4)] + [(kdf, P * c) for c in range(6)] + [(zt, C_KC), (zt, C_VC)])
                for g in range(8):
                    if g >= 2:
                        pe.wait_ge(S[("qT_act", "qT_dve")[g % 2]], 4 * l + g // 2)
                    for c in range(4):
                        t, col = src[4 * g + c]
                        for h in range(TH):
                            mm = pe.transpose(psXc[:, 4 * (g % 2) + c, P * h:P * h + P], t[:, h, col:col + P], ident[:])
                    mm.then_inc(S["qT_psum"], 1)
                pe.wait_ge(S["qT_act"], 4 * l + 4)
                pe.wait_ge(S["qT_dve"], 4 * l + 4)
                pe.wait_ge(S["tile_evac"], tiles[0])
                pe.wait_ge(S["cmp_in"], 16 * 7 * (l + 1))
                pe.transpose(psG[:, 0, 0, 0:64], pe_t[0:64, :], ident[0:64, 0:64]).then_inc(S["pe_psum"], 1)
                a = ATT * l
                for qh in range(TH):
                    d = 2 * l + qh
                    pe.wait_ge(S["attn_out"], a)
                    scores("I", qh, "dots_full")
                    pe.wait_ge(S["relu_on"], d + 1)
                    attend("A", qh, a, 4 * d, None if qh else lambda: compress(l, 0, (0, 1)))
                    attend("B", qh, a + 1, 4 * d + 1, None if qh else lambda: compress(l, 1, (0,)))
                    attend("S", qh, a + 2, 4 * d + 2, None if qh else lambda: compress(l, 1, (1,)))
                    if qh == 0:
                        R.close(4, 1, 2)
                        compress_out(l)
                    attend("W", qh, a + 3, 4 * d + 3)
                    compressed(qh, d, a + 4)
                    a += 5
                pe.wait_ge(S["branch_on"], l + 1)
                for b in range(3):
                    for c in range(4):
                        for h in range(TH):
                            dst = psXc[:, 4 * b + c, :] if b < 2 else psG4[:, c, :]
                            mm = pe.transpose(dst[:, P * h:P * h + P], zt[:, h, (A_G, B_G, C_G)[b] + P * c:
                                                                          (A_G, B_G, C_G)[b] + P * c + P], ident[:])
                mm.then_inc(S["bT_psum"], 1)
                pe.wait_ge(S["bT_act"], l + 1)
                pe.wait_ge(S["bT_dve"], l + 1)
                base = tiles[0]
                for b in range(3):
                    for t in range(2):
                        n = 2 * b + t
                        free_banks(base + n)
                        product((base + n) % 2, (n,), 0, 6, QT[:, 4 * b:4 * b + 4, :], None).then_inc(used, 1)
                tiles[0] += 6
                R.close(6)
                pe.wait_ge(S["up_merged"], l + 1)
                residual(QT[:, 12:20, :])
                pe.wait_ge(S["p_in"], 16 * (l + 1))
                pe.wait_ge(S["x_ready"], 6 + 2 * l)
                for k in range(2):
                    for h in range(TH):
                        mm = pe.transpose(psG[:, 0, 0, T * k + P * h:T * k + P * h + P], PL[:, h, P * k:P * k + P], ident[:])
                mm.then_inc(S["pT2_psum"], 1)
                pe.wait_ge(S["pT2_sb"], l + 1)
                p = page(0, 0, 1)
                w = ring[:, p, :].rearrange("p (a b) -> p a b", b=D)
                for t in range(2):
                    for h in range(TH):
                        for k in range(2):
                            mm = pe.matmul(psG[:, t, h, :], pTs[:, k, P * h:P * h + P], w[:, k, W * t:W * t + W],
                                           start=(k == 0), stop=(k == 1))
                mm.then_inc(used, 1)
                R.close(1)
                tiles[0] += 2
                norm_T(5 + 2 * l)
                pe.wait_ge(S["hT_parted"], 2 * (6 + 2 * l))
                run_parts(2, False)

            pe.wait_ge(S["consts"], N_CONSTS)
            first_layer(0)
            first_layer(1)
            second_layer(0)
            second_layer(1)

        @block.scalar
        def _(act):
            R = Ring()
            tiles = [0]

            def do(dst, src, func, name, **kw):
                act.activation(dst, src, func, **kw).then_inc(S[name], 1)

            def top(k, i=0, pages=0, cols=W):
                p, before = R.at(k, i, pages)
                act.wait_ge(landed[p], R.extra[p] + 16 * before + 16)
                free = R.free(k, i, pages, TOPS)
                if not (isinstance(free, int) and free <= 0):
                    act.wait_ge(used, free)
                do(part_of_page(tops[:, (R.seq + k) % TOPS, :], cols), part_of_page(ring[:, p, :], cols), ACT.Copy, "topped")

            def top_hT(m):
                for g in range(2):
                    act.wait_ge(S["hT_ready"], 2 * m + g + 1)
                    do(hT_top[:, 4 * g:4 * g + 4, :], hT[:, 4 * g:4 * g + 4, :], ACT.Copy, "hT_topped")

            def norm(m):
                act.wait_ge(S["x_ready"], m)
                for h in range(TH):
                    do(htok[:, h, :], x[:, h, :], ACT.Square, "squares", accum_out=st[:, h:h + 1])
                act.wait_ge(S["variance"], m + 1)
                do(st[:, 4:6], st[:, 2:4], ACT.Sqrt, "deviation")

            def row(name, m):
                act.wait_ge(S["x_ready"], m)
                act.dma_start(frow, A[name].rearrange("(o d) -> o d", o=1).to_broadcast([P, D])).then_inc(S["row_in"], 16)
                norm(m)

            def read_out(count, turns, dst, per=2, func=ACT.Copy):
                base, seq = tiles[0], R.seq

                def body(i):
                    for t in range(count):
                        act.wait_ge(used, seq + per * (count * i + t + 1))
                        b = (base + t) % 2
                        d, s = dst(count * i + t, b)
                        act.activation(d, s, func).then_inc(S["tile_evac"], 1)
                if turns == 1:
                    body(0)
                else:
                    with act.Fori(0, turns) as i:
                        body(i)
                tiles[0] += count * turns
                R.close(per * count, turns)

            def read_parts(count, dst, more, func=ACT.Copy, total=None, after=None):
                for t in range(count):
                    for k in (2 * t + 2, 2 * t + 3):
                        if k < 2 * count or more:
                            top(k, cols=min(W, total - k // 2 * W) if total and k < 2 * count else W)
                    act.wait_ge(used, R.seq + 2 * t + 2)
                    d, s = dst(t, (tiles[0] + t) % 2)
                    act.activation(d, s, func).then_inc(S["tile_evac"], 1)
                    if after:
                        after(tiles[0] + t)
                tiles[0] += count
                R.close(2 * count, split=True)

            def feature(b):
                return psG[:, b].rearrange("p a (c t) -> p (a c) t", t=T)

            def exp_keys(l, pair):
                for s in (2 * pair, 2 * pair + 1):
                    act.wait_ge(S["shifted_k"], NSUB * l + s + 1)
                    v = key_buffer(s)[:, :, 0:SUB * (s + 1)]
                    do(v, v, ACT.Exp, "exp_k")

            def constants():
                act.wait_ge(S["lb_max"], 1)
                do(lbt[:, 3:5, :], lbt[:, 1:3, :], ACT.Exp, "init_act")
                act.wait_ge(S["lam_sum"], 1)
                do(lams[:, 4:8], lams[:, 0:4], ACT.Exp, "init_act")
                act.wait_ge(S["angles"], 1)
                do(sinb[:], rr[:, 0:2, :], ACT.Sin, "init_act")
                do(cosb[:], rr[:, 2:4, :], ACT.Sin, "init_act")

            def decays(l, t):
                z_f = zF[:, 8:16, :]
                if t == 1 and l == 0:
                    constants()
                if t == 4:
                    act.wait_ge(S["tile_evac"], 22 * l + 4)
                    do(hd(bF), z_f, ACT.Sigmoid, "f_sig")
                    do(z_f, z_f, ACT.Sigmoid, "z_sig", scale=-1.0)
                if t == 5:
                    do(hd(bQ), w_q, ACT.Sigmoid, "q_sig")
                if t == 6:
                    act.wait_ge(S["f_ready"], l + 1)
                    do(bF, bF, ACT.Ln, "log_f")
                if t == 8:
                    act.wait_ge(S["shifted_q"], l + 1)
                    do(bQ, bQ, ACT.Exp, "exp_q")
                    exp_keys(l, 0)
                if t == 9:
                    act.wait_ge(S["tile_evac"], 22 * l + 8)
                    g = zT[:, :, 1024:2048]
                    do(g, g, ACT.Silu, "silu_g")
                if t in (11, 14, 17):
                    exp_keys(l, t // 3 - 2)

            def recurrence(l):
                act.wait_ge(S["scores_on"], NSUB * l + NSUB)
                do(bF, bC, ACT.Exp, "exp_cum")
                do(eL, hc(bC)[:, :, CH - 1], ACT.Exp, "exp_last")
                act.wait_ge(S["shifted_l"], l + 1)
                do(bK, bK, ACT.Exp, "exp_l")
                gates = zF[:, 40:56, :]
                do(gates, gates, ACT.Sigmoid, "gates_on")
                act.wait_ge(S["klt_psum"], l + 1)
                do(htok_f, psG[:].rearrange("p a b c -> p (a b c)"), ACT.Copy, "klt_sb")
                act.wait_ge(S["o_psum"], l + 1)
                do(o_tok[0:CH], psGf[0:CH], ACT.Copy, "o_act")
                act.wait_ge(S["sub_var"], l + 1)
                do(hst[:], hst[:], ACT.Sqrt, "sub_dev")
                act.wait_ge(S["oT_psum"], l + 1)
                do(oTv, psXc, ACT.Copy, "oT_sb")

            def feed_forward(n, turns, each):
                seq, pages = R.seq, each * PAGES_FFN

                def expert(e, m):
                    at, steps = m * PAGES_FFN, (n + m) * STEPS
                    for j in range(STEPS):
                        here = ffn_page(j, 1)
                        for k in range(2 if j == 0 else ffn_page(j - 1, 1) + 3, here + 3):
                            top(at + k, e, pages)
                        act.wait_ge(used, seq + at + e * pages + here + 1)
                        last = steps + e * each * STEPS + (j - 1 if j == 0 else j - 2) + 1
                        if not (isinstance(last, int) and last <= 0):
                            act.wait_ge(S["hid_on"], last)
                        act.activation(sil[:, j % 2, :], psG[:, j % 2, 0, :], ACT.Silu).then_inc(S["silu_on"], 1)
                    for k in range(PAGES_FFN, PAGES_FFN + 2):
                        top(at + k, e, pages)
                if turns == 1:
                    expert(0, 0)
                else:
                    with act.Fori(0, turns) as e:
                        for m in range(each):
                            expert(e, m)
                R.close(pages, turns, split=True)

            def first_layer(l):
                if l == 0:
                    top(0), top(1)
                norm(2 * l)
                top_hT(2 * l)
                after = lambda n: decays(l, n - 22 * l)
                read_parts(4, lambda t, b: (zF[:, 4 * t:4 * t + 4, :], feature(b)), True, after=after)
                read_parts(4, lambda t, b: (zT[:, :, W * t:W * t + W], psG[:, b]), True, after=after)
                read_parts(10, lambda t, b: (zF[:, 16 + 4 * t:20 + 4 * t, :], feature(b)), False, after=after)
                act.wait_ge(S["tile_evac"], tiles[0])
                recurrence(l)
                read_out(4, 1, lambda t, b: (zF[:, 4 * t:4 * t + 4, :], feature(b)))
                R.close(4)
                top(0), top(1)
                norm(2 * l + 1)
                top_hT(2 * l + 1)
                if l:
                    act.wait_ge(S["top_diff"], 1)
                    do(lg[:, 4, 0:2], lg[:, 3, 0:2], ACT.Exp, "top_exp")
                feed_forward(l, *((EXPERTS // 2, 2) if l else (1, 1)))

            def softmax(n, keys):
                act.wait_ge(S["scores_cut"], n + 1)
                for s in range(8):
                    act.activation(sv[:, s, 0:keys], sv[:, s, 0:keys], ACT.Exp, bias=mx[:, s:s + 1], scale=SCALE,
                                   accum_out=den[:, s:s + 1]).then_inc(S["exp_on"], 1)
                act.wait_ge(S["pT_psum"], n + 1)
                do(PT[:, 0], psGf[:, 0, :].rearrange("p (s q) -> p s q", q=P), ACT.Copy, "pT_act")

            def second_layer(l):
                if l:
                    top(0), top(1)
                norm(5 + 2 * l)
                top_hT(4 + 2 * l)
                read_parts(11, lambda t, b: (zt[:, :, W * t:min(W * t + W, Z_COLS)], psG[:, b, :, 0:min(W, Z_COLS - W * t)]),
                           True, total=Z_COLS)
                read_parts(6, lambda t, b: (zm[:, 4 * t:4 * t + 4, :], feature(b)), False, func=ACT.Sigmoid)
                for col in (A_G, B_G, C_G):
                    do(zt[:, :, col:col + W], zt[:, :, col:col + W], ACT.Silu, "branch_gates")
                do(bgs[:], zt[:, :, C_BG:C_BG + 24], ACT.Sigmoid, "branch_gates")
                for g in range(0, 8, 2):
                    act.wait_ge(S["qT_psum"], 8 * l + g + 1)
                    do(QT[:, 4 * g:4 * g + 4, :], psXc[:, 0:4, :], ACT.Copy, "qT_act")
                for qh in range(TH):
                    d, keys = 2 * l + qh, P * (qh + 1)
                    act.wait_ge(S["dots_full"], d + 1)
                    act.wait_ge(S["qT_dve"], 4 * l + 4)
                    if qh:
                        act.wait_ge(S["attn_out"], ATT * l + 5)
                    do(sv[:, :, 0:keys], psXc[:, :, 0:keys], ACT.Relu, "relu_on", scale=HD ** -0.5)
                    softmax(4 * d, keys)
                    act.wait_ge(S["sub2_var"], d + 1)
                    do(lg[:, 6, 0:4], lg[:, 5, 0:4], ACT.Sqrt, "sub2_dev")
                    softmax(4 * d + 1, keys)
                    softmax(4 * d + 2, keys)
                    if qh == 0:
                        act.wait_ge(used, R.seq + 4)
                        R.close(4, 1, 2)
                        do(gel[:].rearrange("p (n g) m -> p n g m", g=2)[:, :, :, 0:NCMP], cmp_h[:, :, :, 0:NCMP],
                           ACT.Gelu_apprx_tanh, "gelu_on")
                    softmax(4 * d + 3, keys)
                    act.wait_ge(S["cs_cut"], d + 1)
                    do(pc[:, :, 0:NCMP], pc[:, :, 0:NCMP], ACT.Exp, "cs_exp", scale=SCALE)
                    act.wait_ge(S["pcT_psum"], d + 1)
                    do(pcT[:], psG[:, 0, 0, 0:256].rearrange("p (a q) -> p a q", a=2), ACT.Copy, "pcT_sb")
                act.wait_ge(S["bT_psum"], l + 1)
                do(QT[:, 0:8, :], psXc, ACT.Copy, "bT_act")
                R.close(6)
                R.close(4)
                tiles[0] += 6
                act.wait_ge(S["x_ready"], 6 + 2 * l)
                act.dma_start(PL, A["p_2"][l, 0].rearrange("(h p) d -> p h d", p=P)).then_inc(S["p_in"], 16)
                act.wait_ge(S["pT2_psum"], l + 1)
                do(pTs, psG[:, 0, 0, :].rearrange("p (k t) -> p k t", k=2), ACT.Copy, "pT2_sb")
                act.wait_ge(used, R.seq + 1)
                R.close(1)
                for t in range(2):
                    do(pl[:, :, W * t:W * t + W], psG[:, t], ACT.Copy, "tile_evac")
                tiles[0] += 2
                top(0), top(1)
                norm(6 + 2 * l)
                top_hT(5 + 2 * l)
                read_parts(2, lambda t, b: (plg[:, :, W * t:W * t + W], psG[:, b]), False, func=ACT.Sigmoid)

            act.wait_ge(S["x_in"], 32)
            first_layer(0)
            first_layer(1)
            row("final_norm", 4)
            second_layer(0)
            second_layer(1)
            row("final_norm_g_2", 9)

        @block.gpsimd
        def _(pool):
            n_of = {}

            def step(ins, name="pool_step"):
                ins.then_inc(S[name], 1)
                n_of[name] = n_of.get(name, 0) + 1
                pool.wait_ge(S[name], n_of[name])

            step(pool.memset(ones[:], 1.0))
            step(pool.memset(ident[:], 0.0))
            step(pool.affine_select(out=ident[:], in_=ident[:], compare_op=ALU.not_equal, fill=1.0, base=0,
                                    pattern=[[-1, P]], channel_multiplier=1), "consts")
            step(pool.memset(caus[:], 0.0))
            step(pool.affine_select(out=caus[:], in_=caus[:], compare_op=ALU.is_ge, fill=NEG, base=0,
                                    pattern=[[-1, P]], channel_multiplier=1), "consts")
            step(pool.memset(cm01[:], 1.0))
            step(pool.memset(cmask[:], 0.0))
            step(pool.affine_select(out=cm01[:], in_=cm01[:], compare_op=ALU.is_ge, fill=0.0, base=-31,
                                    pattern=[[P, TH], [-16, 16]], channel_multiplier=1), "consts")
            step(pool.affine_select(out=cmask[:], in_=cmask[:], compare_op=ALU.is_ge, fill=NEG, base=-31,
                                    pattern=[[P, TH], [-16, 16]], channel_multiplier=1), "consts")
            step(pool.memset(smask[:], 1))
            for at in (0, CH):
                step(pool.affine_select(out=smask[at:at + CH], in_=smask[at:at + CH], compare_op=ALU.is_ge, fill=0.0,
                                        base=0, pattern=[[1, CH]], channel_multiplier=-1), "consts")
            step(pool.memset(reset[:], 1.0))
            step(pool.memset(reset[:].rearrange("p (c t) -> p c t", t=CH)[:, :, 0:1], 0.0), "consts")
            step(pool.memset(sTm[:], 0.0), "consts")
            step(pool.memset(pc[:], 0.0))
            step(pool.memset(hidc[:], 0.0), "consts")

            R = Ring()
            for l in range(2):
                pool.wait_ge(S["hT_ready"], 4 * l + 2)
                step(pool.memset(bK, 0.0), "ka_zero")
                pool.wait_ge(S["tile_evac"], 22 * l + 18)
                tmp = hT[:]

                def tap(j):
                    return bc(cw[:, l, j, :].unsqueeze(2), KD, T)

                pool.wait_ge(params, 16 * N_PARAMS)
                step(pool.tensor_tensor(w_b, w_b, w_u, ALU.mult))
                step(pool.tensor_tensor(w_u, w_b, tap(2), ALU.mult))
                for j, back in ((1, 1), (0, 2)):
                    step(pool.tensor_tensor(tmp, w_b, tap(j), ALU.mult))
                    step(pool.tensor_tensor(w_u[:, :, back:T], w_u[:, :, back:T], tmp[:, :, 0:T - back], ALU.add))
                step(pool.tensor_tensor(w_u, w_u, w_c, ALU.mult), "conv_ready")
                R.close(36, split=True), R.close(12)
                R.close(EXPERTS * PAGES_FFN if l else PAGES_FFN, split=True)

            for l in range(2):
                R.close(22, split=True)
                pool.wait_ge(S["parted"], R.parts + 2)
                for k in range(2, 6):
                    n = R.seq + k
                    pool.wait_ge(S["topped"], R.parts + k + 1)
                    pool.tensor_tensor(ring_rest[:, n % NP, :], ring[:, n % NP, :], tops[:, n % TOPS, :].bitcast(F32),
                                       ALU.subtract).then_inc(S["parted"], 1)
                    pool.wait_ge(S["parted"], R.parts + k + 1)
                R.close(12, split=True)
                R.close(15)
                R.close(4, split=True)

        @block.vector
        def _(dve):
            R = Ring()
            n_of = {}
            tiles = [0]

            def go(ins, name="dve_step"):
                ins.then_inc(S[name], 1)
                n_of[name] = n_of.get(name, 0) + 1

            def own(name="dve_step"):
                dve.wait_ge(S[name], n_of[name])

            def step(ins, name="dve_step"):
                go(ins, name)
                own(name)

            def norm(m, n=None, gain=None):
                dve.wait_ge(S["squares"], 2 * m + 2)
                step(dve.tensor_scalar(st[:, 2:4], st[:, 0:2], 1.0 / D, EPS, ALU.mult, ALU.add), "variance")
                dve.wait_ge(S["deviation"], m + 1)
                step(dve.reciprocal(st[:, 6:8], st[:, 4:6]))
                if gain is None:
                    dve.wait_ge(S["row_in"], 16 * (1 if m == 4 else 2))
                    for h in range(TH):
                        step(dve.scalar_tensor_tensor(out=x[:, h, :], in0=x[:, h, :], scalar=st[:, 6 + h:7 + h], in1=frow,
                                                      op0=ALU.mult, op1=ALU.mult))
                    step(dve.tensor_copy(st[:, 8:9], st[:, 6:7]), "x_ready")
                    return
                for h in range(TH):
                    step(dve.tensor_scalar(htok[:, h, :], x[:, h, :], st[:, 6 + h:7 + h], None, ALU.mult), "h_scaled")
                dve.wait_ge(S["hT_psum"], n + 1)
                halves = [slice(4 * g, 4 * g + 4) for g in range(2)]
                for f in halves:
                    go(dve.tensor_tensor(hT[:, f, :], psXc[:, f, :], bc(gains[:, gain, f].unsqueeze(2), 4, T), ALU.mult), "hT_ready")
                own("hT_ready")
                if n == 3:
                    dve.wait_ge(S["logits"], 1)
                for g, f in enumerate(halves):
                    dve.wait_ge(S["hT_topped"], n_of.get("hT_parted", 0) + 1)
                    go(dve.tensor_tensor(hT_rest[:, f, :], hT[:, f, :], hT_top[:, f, :].bitcast(F32), ALU.subtract), "hT_parted")

            def rest(k, i=0, pages=0, cols=W):
                n = R.seq + k
                p, u = n % NP, n % TOPS
                dve.wait_ge(S["topped"], R.parts + k + i * pages + 1)
                dve.tensor_tensor(part_of_page(ring_rest[:, p, :], cols), part_of_page(ring[:, p, :], cols),
                                  part_of_page(tops[:, u, :].bitcast(F32), cols), ALU.subtract).then_inc(S["parted"], 1)

            def rests(pages, more, total=None, after=None):
                for k in range(2, pages + 2 * more):
                    rest(k, cols=min(W, total - k // 2 * W) if total and k < pages else W)
                    if after and k % 2:
                        after(k // 2 - 1)
                if after and not more:
                    after(pages // 2 - 1)
                R.close(pages, split=True)

            def residual():
                for t in range(2):
                    dve.wait_ge(used, R.seq + 2 * t + 2)
                    step(dve.tensor_tensor(x[:, :, W * t:W * t + W], x[:, :, W * t:W * t + W], psG[:, t], ALU.add),
                         "x_ready" if t else "dve_step")
                R.close(4)

            def constants():
                dve.wait_ge(params, 16 * N_PARAMS)
                B = lambda i: lbt[:, i, :]
                step(dve.tensor_tensor(B(0), lbr[:, 0, :], lbr[:, 1, :], ALU.max))
                go(dve.tensor_tensor(B(1), lbr[:, 0, :], B(0), ALU.subtract))
                go(dve.tensor_tensor(B(2), lbr[:, 1, :], B(0), ALU.subtract))
                own()
                step(dve.tensor_copy(st[:, 10:11], ones[:, 0:1]), "lb_max")
                for l in range(2):
                    for n in range(2):
                        a = lamr[:, l, 128 * n:128 * n + 64]
                        step(dve.tensor_tensor(a, a, lamr[:, l, 128 * n + 64:128 * n + 128], ALU.mult))
                        step(dve.tensor_reduce(lams[:, 2 * l + n:2 * l + n + 1], a, AX_X, ALU.add))
                step(dve.tensor_copy(st[:, 10:11], ones[:, 0:1]), "lam_sum")
                step(dve.tensor_copy(posf[:], posi[:]))
                for j in range(ROT):
                    go(dve.memset(inv[:, j:j + 1], float(np.float32(THETA) ** np.float32(-2.0 * j / (2 * ROT)))))
                own()
                for h in range(TH):
                    step(dve.tensor_scalar(ang[:, h, :], inv[:], posf[:, h:h + 1], None, ALU.mult))
                for q in range(2):
                    r, t = rr[:, 2 * q:2 * q + 2, :], tq[:]
                    step(dve.tensor_scalar(t, ang[:], 1.0 / (2 * math.pi), 0.25 * q, ALU.mult, ALU.add))
                    step(dve.tensor_scalar(t, t, ROUND, None, ALU.add))
                    step(dve.tensor_scalar(t, t, -ROUND, None, ALU.add))
                    step(dve.scalar_tensor_tensor(out=r, in0=t, scalar=-PI2[0], in1=ang[:], op0=ALU.mult, op1=ALU.add))
                    for part in PI2[1:]:
                        step(dve.scalar_tensor_tensor(out=r, in0=t, scalar=-part, in1=r, op0=ALU.mult, op1=ALU.add))
                    if q:
                        step(dve.tensor_scalar(r, r, math.pi / 2, None, ALU.add))
                    step(dve.tensor_scalar(r, r, PI_UP, -PI_UP, ALU.min, ALU.max))
                step(dve.tensor_copy(st[:, 10:11], ones[:, 0:1]), "angles")
                dve.wait_ge(S["init_act"], 4)
                step(dve.tensor_tensor(B(0), B(3), B(4), ALU.add))
                step(dve.reciprocal(B(5), B(0)))
                go(dve.tensor_tensor(B(1), B(3), B(5), ALU.mult))
                go(dve.tensor_tensor(B(2), B(4), B(5), ALU.mult))
                own()
                step(dve.tensor_tensor(B(2), B(1), B(2), ALU.add))
                go(dve.tensor_tensor(lbT[:, 0, :], B(1), B(1), ALU.subtract))
                go(dve.tensor_tensor(lbT[:, 1, :], B(2), B(1), ALU.subtract))
                own()
                step(dve.tensor_scalar(oml[:], lbT[:], -1.0, 1.0, ALU.mult, ALU.add))
                for l in range(2):
                    init = 0.8 - 0.6 * math.exp(-0.3 * l)
                    step(dve.tensor_tensor(nlam[:, l:l + 1], lams[:, 5 + 2 * l:6 + 2 * l], lams[:, 4 + 2 * l:5 + 2 * l], ALU.subtract))
                    step(dve.tensor_scalar(nlam[:, l:l + 1], nlam[:, l:l + 1], -init, None, ALU.add))
                    step(dve.tensor_scalar(sg2[:, l, :], sg2[:, l, :], 1.0 - init, None, ALU.mult))

            def shift(l, s):
                if s >= 2:
                    dve.wait_ge(S["scores_on"], NSUB * l + s - 1)
                w, at = SUB * (s + 1), SUB * s + SUB // 2 - 1
                cum = hc(bC)
                go(dve.tensor_tensor(key_buffer(s)[:, :, 0:w], bc(cum[:, :, at:at + 1], HEADS * NC, w), cum[:, :, 0:w],
                                     ALU.subtract), "shifted_k")

            def anchored_keys(l, s):
                w = SUB * (s + 1)
                v = key_buffer(s)[:, :, 0:w]
                dve.wait_ge(S["exp_k"], NSUB * l + s + 1)
                step(dve.tensor_tensor(v, v, w_k.rearrange("p h (c t) -> p (h c) t", t=CH)[:, :, 0:w], ALU.mult), "ka_on")

            def decays(l, t):
                if t == 1 and l == 0:
                    constants()
                if t == 5:
                    dve.wait_ge(S["f_sig"], l + 1)
                    step(dve.tensor_tensor(hd(bF), hd(bF), bc(oml[:, l, :].unsqueeze(2), HEADS, T), ALU.mult))
                    step(dve.tensor_tensor(hd(bF), hd(bF), bc(lbT[:, l, :].unsqueeze(2), HEADS, T), ALU.add))
                    step(dve.tensor_scalar(bF, bF, F_MIN, None, ALU.max), "f_ready")
                if t == 6:
                    dve.wait_ge(S["q_sig"], l + 1)
                    step(dve.scalar_tensor_tensor(out=w_q, in0=w_q, scalar=float(P) ** -0.5, in1=hd(bQ), op0=ALU.mult, op1=ALU.mult))
                    dve.wait_ge(S["z_sig"], l + 1)
                    step(dve.tensor_tensor(w_k, w_k, bc(oml[:, l, :].unsqueeze(2), HEADS, T), ALU.mult))
                if t == 7:
                    dve.wait_ge(S["log_f"], l + 1)
                    for h in range(HEADS):
                        go(dve.tensor_tensor_scan(hd(bC)[:, h, :], reset[:], hd(bF)[:, h, :], 0.0, ALU.mult, ALU.add))
                    own()
                    sub = lambda b: b.rearrange("p (n r) -> p n r", r=SUB)
                    step(dve.tensor_tensor(sub(bQ), sub(bC), bc(sub(bC)[:, :, SUB // 2 - 1:SUB // 2], T, SUB), ALU.subtract),
                         "shifted_q")
                    dve.wait_ge(S["ka_zero"], l + 1)
                if t == 9:
                    dve.wait_ge(S["exp_q"], l + 1)
                    step(dve.tensor_tensor(hd(bQ), hd(bQ), w_q, ALU.mult), "qa_on")
                for pair, first in enumerate((7, 11, 14, 17)):
                    for s in (2 * pair, 2 * pair + 1):
                        if t == first:
                            shift(l, s)
                for pair, second in enumerate((9, 12, 15, 17)):
                    for s in (2 * pair, 2 * pair + 1):
                        if t == second:
                            anchored_keys(l, s)

            def recurrence(l):
                cum = hc(bC)
                dve.wait_ge(S["scores_on"], NSUB * l + 7)
                step(dve.tensor_tensor(hc(bK), bc(cum[:, :, CH - 1:CH], HEADS * NC, CH), cum, ALU.subtract), "shifted_l")
                dve.wait_ge(S["exp_cum"], l + 1)
                step(dve.tensor_tensor(hd(bF), hd(bF), w_q, ALU.mult), "qe_on")
                dve.wait_ge(S["exp_l"], l + 1)
                step(dve.tensor_tensor(hd(bK), hd(bK), w_k, ALU.mult), "kl_on")
                dve.wait_ge(S["scores_on"], NSUB * l + 8)
                step(dve.copy_predicated(sTm[:], bc(smask[:].unsqueeze(1), 16, CH), psXs), "s_masked")
                dve.wait_ge(S["exp_last"], l + 1)
                e4 = eL[:].rearrange("p (h c) -> p h c", c=NC)
                for c in range(3):
                    dve.wait_ge(S["u_on"], 3 * l + c + 1)
                    u = (psGf[:, c, :] if c < 2 else psX[:, 2:4, :].rearrange("p a b -> p (a b)")).rearrange(
                        "p (h d) -> p h d", d=P)
                    if c == 0:
                        step(dve.tensor_copy(states[1], u), "states_on")
                    else:
                        step(dve.tensor_tensor(states[c + 1], states[c], bc(e4[:, :, c:c + 1], HEADS, P), ALU.mult))
                        step(dve.tensor_tensor(states[c + 1], states[c + 1], u, ALU.add), "states_on")
                dve.wait_ge(S["o_psum"], l + 1)
                step(dve.tensor_copy(o_tok[CH:P], psX[CH:P].rearrange("p (h a) b -> p h (a b)", h=TH)), "o_dve")
                dve.wait_ge(S["o_act"], l + 1)
                o16 = bK.rearrange("p (n d) -> p n d", d=P)
                q16 = bQ.rearrange("p (n d) -> p n d", d=P)
                step(dve.tensor_tensor(bQ, bK, bK, ALU.mult))
                step(dve.tensor_reduce(hst[:], q16, AX_X, ALU.add))
                step(dve.tensor_scalar(hst[:], hst[:], 1.0 / P, EPS, ALU.mult, ALU.add), "sub_var")
                dve.wait_ge(S["sub_dev"], l + 1)
                step(dve.reciprocal(hst2[:], hst[:]))
                step(dve.tensor_tensor(o16, o16, bc(hst2[:].unsqueeze(2), 16, P), ALU.mult))
                step(dve.tensor_tensor(o16, o16, bc(gn[:, l, :].unsqueeze(1), 16, P), ALU.mult))
                dve.wait_ge(S["silu_g"], l + 1)
                step(dve.tensor_tensor(o_tok, o_tok, zT[:, :, 1024:2048], ALU.mult), "o_on")

            def feed_forward(n, turns, each, gated):
                seq, pages = R.seq, each * PAGES_FFN

                def expert(e, m):
                    at, steps = m * PAGES_FFN, (n + m) * STEPS
                    for j in range(STEPS):
                        for k in range(2 if j == 0 else ffn_page(j - 1, 1) + 3, ffn_page(j, 1) + 3):
                            rest(at + k, e, pages)
                        now = steps + e * each * STEPS + j + 1
                        dve.wait_ge(S["silu_on"], now)
                        dve.tensor_tensor(hid[:, j % 2, :], sil[:, j % 2, :], psG[:, j % 2, 1, :], ALU.mult).then_inc(S["hid_on"], 1)
                        if j >= 2:
                            dve.wait_ge(used, seq + at + e * pages + ffn_page(j - 2, 2) + 1)
                        elif j == 0:
                            dve.wait_ge(used, seq + at + e * pages)
                        dve.wait_ge(S["hid_on"], now)
                        top = hid_top[:, j % 2].rearrange("p k t -> p (k t)")
                        dve.tensor_copy(top, hid[:, j % 2, :]).then_inc(S["hid_topped"], 1)
                        dve.wait_ge(S["hid_topped"], now)
                        dve.tensor_tensor(hid_rest[:, j % 2].rearrange("p k t -> p (k t)"), hid[:, j % 2, :], top.bitcast(F32),
                                          ALU.subtract).then_inc(S["hid_parted"], 1)
                    for k in range(PAGES_FFN, PAGES_FFN + 2):
                        rest(at + k, e, pages)
                    dve.wait_ge(used, seq + at + e * pages + PAGES_FFN)
                    done = 2 * (n + m + each * e)
                    if not (isinstance(done, int) and done == 0):
                        dve.wait_ge(S["y_added"], done)
                    for h in range(TH):
                        y = psX[:, 2 * h:2 * h + 2, :].rearrange("p a b -> p (a b)")
                        if gated:
                            ins = dve.scalar_tensor_tensor(out=x[:, h, :], in0=y, scalar=gate[:, h, bass.ds(2 * e + m, 1)],
                                                           in1=x[:, h, :], op0=ALU.mult, op1=ALU.add)
                        else:
                            ins = dve.tensor_tensor(x[:, h, :], y, x[:, h, :], ALU.add)
                        ins.then_inc(S["y_added"], 1)
                if turns == 1:
                    expert(0, 0)
                else:
                    with dve.Fori(0, turns) as e:
                        for m in range(each):
                            expert(e, m)
                dve.wait_ge(S["y_added"], 2 * (n + turns * each))
                step(dve.tensor_copy(st[:, 9:10], st[:, 6:7]), "x_ready")
                R.close(pages, turns, split=True)

            def route():
                dve.wait_ge(S["logits"], 1)
                L = lambda i: lg[:, i, :]
                for h in range(TH):
                    step(dve.tensor_copy(L(h), psX[:, h, 0:EXPERTS]), "dve_step")
                step(dve.tensor_copy(st[:, 10:11], st[:, 6:7]), "lg_read")
                for h in range(TH):
                    step(dve.max(out=L(7 + h), in_=L(h)))
                    step(dve.tensor_tensor(lg[:, 3, h:h + 1], lg[:, 7 + h, 1:2], lg[:, 7 + h, 0:1], ALU.subtract))
                step(dve.tensor_copy(st[:, 10:11], st[:, 6:7]), "top_diff")
                dve.wait_ge(S["top_exp"], 1)
                step(dve.tensor_scalar(lg[:, 4, 2:4], lg[:, 4, 0:2], 1.0, None, ALU.add))
                step(dve.reciprocal(lg[:, 4, 4:6], lg[:, 4, 2:4]))
                step(dve.tensor_tensor(lg[:, 4, 6:8], lg[:, 4, 4:6], lg[:, 4, 0:2], ALU.mult))
                for h in range(TH):
                    second = lg[:, 7 + h, 1:2]
                    step(dve.tensor_scalar(L(2), L(h), second, None, ALU.is_gt))
                    step(dve.tensor_reduce(lg[:, 9, 0:1], L(2), AX_X, ALU.add))
                    step(dve.tensor_scalar(L(5), L(h), second, None, ALU.is_equal))
                    step(dve.tensor_tensor_scan(L(6), ones[:, 0:EXPERTS], L(5), 0.0, ALU.mult, ALU.add))
                    step(dve.tensor_scalar(L(6), L(6), lg[:, 9, 0:1], 2.0, ALU.add, ALU.is_le))
                    step(dve.tensor_tensor(L(5), L(5), L(6), ALU.mult))
                    step(dve.tensor_scalar(L(2), L(2), lg[:, 4, 4 + h:5 + h], None, ALU.mult))
                    step(dve.scalar_tensor_tensor(out=gate[:, h, :], in0=L(5), scalar=lg[:, 4, 6 + h:7 + h], in1=L(2),
                                                  op0=ALU.mult, op1=ALU.add))

            def first_layer(l):
                if l == 0:
                    rest(0), rest(1)
                norm(2 * l, 2 * l, 0 + l)
                rests(36, False, after=lambda t: decays(l, t))
                recurrence(l)
                base = tiles[0] = 22 * l
                dve.wait_ge(S["tile_evac"], base + 22)
                dve.wait_ge(S["gates_on"], l + 1)
                R.close(8)
                step(dve.tensor_tensor(w_q, w_q, zF[:, 40:48, :], ALU.mult))
                step(dve.tensor_tensor(w_k, w_k, zF[:, 48:56, :], ALU.mult))
                step(dve.tensor_tensor(w_q, w_q, w_k, ALU.add), "merged")
                residual()
                rest(0), rest(1)
                norm(2 * l + 1, 2 * l + 1, 2 + l)
                if l:
                    route()
                feed_forward(l, *((EXPERTS // 2, 2) if l else (1, 1)), bool(l))

            def rope(v, heads):
                lo, hi = v[:, :, :, 0:ROT], v[:, :, :, ROT:2 * ROT]
                c = bc(cosb[:].unsqueeze(2), TH, heads, ROT)
                s = bc(sinb[:].unsqueeze(2), TH, heads, ROT)
                t = [rt[:, n, 0:TH * heads * ROT].rearrange("p (h n d) -> p h n d", h=TH, d=ROT) for n in range(4)]
                go(dve.tensor_tensor(t[0], lo, c, ALU.mult))
                go(dve.tensor_tensor(t[1], hi, s, ALU.mult))
                go(dve.tensor_tensor(t[2], hi, c, ALU.mult))
                go(dve.tensor_tensor(t[3], lo, s, ALU.mult))
                own()
                go(dve.tensor_tensor(lo, t[0], t[1], ALU.subtract))
                go(dve.tensor_tensor(hi, t[2], t[3], ALU.add))
                own()

            def by_head(t, col, heads):
                return t[:, :, col:col + 64 * heads].rearrange("p h (n d) -> p h n d", d=64)

            bg = lambda qh, n: bgs[:, qh, :].rearrange("p (c q r) -> p q c r", q=2, r=3)[:, :, :, n]
            slots = lambda v: v.rearrange("p (q c) -> p q c", q=2)
            by_slot = lambda v: v.rearrange("p (c q d) -> p q c d", q=2, d=64)
            flat = osum.rearrange("p s d -> p (s d)")

            def softmax_in(kind, qh, n):
                keys = P * (qh + 1)
                dve.wait_ge(S["scores_full"], n + 1)
                if kind == "B":
                    go(dve.tensor_tensor(sv[:, :, 0:keys], psXc[:, :, 0:keys], bc(bias[:, 0:keys].unsqueeze(1), 8, keys), ALU.add))
                else:
                    if qh:
                        go(dve.tensor_copy(sv[:, :, 0:P], psXc[:, :, 0:P]))
                    go(dve.tensor_tensor(sv[:, :, P * qh:keys], psXc[:, :, P * qh:keys], bc(caus[:].unsqueeze(1), 8, P), ALU.add))
                own()
                step(dve.tensor_reduce(mx[:], sv[:, :, 0:keys], AX_X, ALU.max))
                step(dve.tensor_scalar(mx[:], mx[:], -SCALE, None, ALU.mult), "scores_cut")

            def softmax_out(qh, n):
                dve.wait_ge(S["exp_on"], 8 * n + 8)
                step(dve.reciprocal(rden[:], den[:]))
                if qh:
                    dve.wait_ge(S["pT_psum"], n + 1)
                    step(dve.tensor_copy(PT[:, 1], psGf[:, 1, :].rearrange("p (s q) -> p s q", q=P)), "pT_dve")

            def index(l, qh, d):
                keys = P * (qh + 1)
                dve.wait_ge(S["relu_on"], d + 1)
                for s in range(8):
                    head = 2 * (s % 4) + s // 4
                    if s == 0:
                        step(dve.tensor_scalar(score[:, 0:keys], sv[:, s, 0:keys], iws[:, qh, head:head + 1], None, ALU.mult))
                    else:
                        step(dve.scalar_tensor_tensor(out=score[:, 0:keys], in0=sv[:, s, 0:keys], scalar=iws[:, qh, head:head + 1],
                                                      in1=score[:, 0:keys], op0=ALU.mult, op1=ALU.add))
                step(dve.tensor_tensor(score[:, P * qh:keys], score[:, P * qh:keys], caus[:], ALU.add))

            def best(qh):
                keys = P * (qh + 1)
                src = score
                for r in range(K_SEL // 8):
                    step(dve.max(out=m8[:], in_=src[:, 0:keys]))
                    step(dve.match_replace(out=(work, score)[r % 2][:, 0:keys], in_to_replace=m8[:], in_values=src[:, 0:keys],
                                           imm_value=TAKEN))
                    src = (work, score)[r % 2]
                step(dve.tensor_scalar(bias[:, 0:keys], src[:, 0:keys], TAKEN, 1.0, ALU.is_equal, ALU.subtract))
                step(dve.tensor_scalar(bias[:, 0:keys], bias[:, 0:keys], -NEG, None, ALU.mult))
                step(dve.tensor_tensor(bias[:, P * qh:keys], bias[:, P * qh:keys], caus[:], ALU.add))

            def attend(kind, l, qh, n, meanwhile=None):
                softmax_in(kind, qh, n)
                if meanwhile:
                    meanwhile()
                softmax_out(qh, n)
                dve.wait_ge(S["av_full"], n + 1)
                ps = psX[:].rearrange("p a b -> p (a b)")
                dve.wait_ge(S["branch_gates"], 4 * l + 4)
                if kind == "A":
                    step(dve.tensor_tensor(osum, ps[:, 0:1024].rearrange("p (s d) -> p s d", d=P), bc(rden[:].unsqueeze(2), 8, P), ALU.mult))
                    o, sq = osum[:, 0:4, :], osum[:, 4:8, :]
                    step(dve.scalar_tensor_tensor(out=o, in0=sq, scalar=nlam[:, l:l + 1], in1=o, op0=ALU.mult, op1=ALU.add))
                    step(dve.tensor_tensor(sq, o, o, ALU.mult))
                    step(dve.tensor_reduce(lg[:, 9, 0:4], sq, AX_X, ALU.add))
                    step(dve.tensor_scalar(lg[:, 5, 0:4], lg[:, 9, 0:4], 1.0 / P, EPS, ALU.mult, ALU.add), "sub2_var")
                    dve.wait_ge(S["sub2_dev"], 2 * l + qh + 1)
                    step(dve.reciprocal(lg[:, 7, 0:4], lg[:, 6, 0:4]))
                    step(dve.tensor_tensor(o, o, bc(lg[:, 7, 0:4].unsqueeze(2), 4, P), ALU.mult))
                    step(dve.tensor_tensor(o, o, bc(sg2[:, l, :].unsqueeze(1), 4, P), ALU.mult))
                    gated = zt[:, qh, A_G:A_G + W]
                    step(dve.tensor_tensor(gated, gated, flat[:, 0:W], ALU.mult), "attn_out")
                    return
                o = ps[:, 0:W].rearrange("p (q c d) -> p q c d", q=2, d=64)
                if kind != "B":
                    step(dve.tensor_tensor(slots(rden[:]), slots(rden[:]), bg(qh, 1 if kind == "S" else 2), ALU.mult))
                step(dve.tensor_tensor(by_slot(flat[:, 0:W]), o, bc(slots(rden[:]).unsqueeze(3), 2, 4, 64), ALU.mult))
                if kind == "B":
                    gated = zt[:, qh, B_G:B_G + W]
                    step(dve.tensor_tensor(gated, gated, flat[:, 0:W], ALU.mult), "attn_out")
                elif kind == "S":
                    step(dve.tensor_copy(flat[:, W:2 * W], flat[:, 0:W]), "attn_out")
                else:
                    step(dve.tensor_tensor(flat[:, W:2 * W], flat[:, W:2 * W], flat[:, 0:W], ALU.add), "attn_out")

            def compressed(l, qh, d):
                dve.wait_ge(S["cs_full"], d + 1)
                v = pc[:, :, 0:NCMP]
                ps = psX[:, 0:2, 0:64].rearrange("p q (c n) -> p q c n", n=16)[:, :, :, 0:NCMP]
                v4 = v.rearrange("p (q c) n -> p q c n", q=2)
                cm = cmask[:, qh, 0:NCMP].unsqueeze(1).unsqueeze(1)
                step(dve.tensor_tensor(v4, ps, bc(cm, 2, 4, NCMP), ALU.add))
                step(dve.tensor_reduce(mx[:], v, AX_X, ALU.max))
                step(dve.tensor_tensor(v, v, bc(mx[:].unsqueeze(2), 8, NCMP), ALU.subtract), "cs_cut")
                dve.wait_ge(S["cs_exp"], d + 1)
                step(dve.tensor_reduce(den[:], v, AX_X, ALU.add))
                step(dve.reciprocal(rden[:], den[:]))
                step(dve.tensor_tensor(slots(rden[:]), slots(rden[:]), bg(qh, 0), ALU.mult))
                step(dve.tensor_tensor(v, v, bc(cm01[:, qh, 0:NCMP].unsqueeze(1), 8, NCMP), ALU.mult), "cs_norm")
                dve.wait_ge(S["cav_full"], d + 1)
                out4 = flat[:, 0:W].rearrange("p (c q d) -> p c q d", q=2, d=64)
                step(dve.tensor_tensor(out4, psX[:, :, 0:P].rearrange("p c (q d) -> p c q d", q=2),
                                       bc(slots(rden[:]).rearrange("p q c -> p c q").unsqueeze(3), 4, 2, 64), ALU.mult))
                step(dve.tensor_tensor(flat[:, W:2 * W], flat[:, W:2 * W], flat[:, 0:W], ALU.add))
                gated = zt[:, qh, C_G:C_G + W]
                step(dve.tensor_tensor(gated, gated, flat[:, W:2 * W], ALU.mult), "attn_out")

            def second_layer(l):
                base = tiles[0]
                if l:
                    rest(0), rest(1)
                norm(5 + 2 * l, 4 + 2 * l, 4 + l)
                rests(22, True, Z_COLS)
                dve.wait_ge(S["tile_evac"], base + 11)
                step(dve.tensor_copy(crt, zt[:, :, C_Q:C_Q + W]))
                for t, col, heads in ((zt, A_Q, 16), (zt, B_Q, 9), (zt, I_Q, 9), (crt, 0, 8), (zt, C_KS, 2), (zt, C_KW, 2)):
                    rope(by_head(t, col, heads), heads)
                for w, col in enumerate((B_K, I_K, C_KS, C_KS + 64, C_KW, C_KW + 64)):
                    go(dve.tensor_copy(kdup[:, :, w, :].rearrange("p h (u d) -> p h u d", u=2),
                                       bc(zt[:, :, col:col + 64].unsqueeze(2), TH, 2, 64)))
                go(dve.tensor_scalar(iws[:], zt[:, :, I_W:I_W + 8], 8.0 ** -0.5, None, ALU.mult))
                own()
                step(dve.tensor_copy(st[:, 10:11], st[:, 6:7]), "rope_on")
                tiles[0] += 17
                dve.wait_ge(S["parted"], R.parts + 6)
                for k in range(6, 12):
                    rest(k)
                R.close(12, split=True)
                for g in range(1, 8, 2):
                    dve.wait_ge(S["qT_psum"], 8 * l + g + 1)
                    step(dve.tensor_copy(QT[:, 4 * g:4 * g + 4, :], psXc[:, 4:8, :]), "qT_dve")
                dve.wait_ge(S["pe_psum"], l + 1)
                step(dve.tensor_copy(peT[:], psG[:, 0, 0, 0:64].rearrange("p (n r) -> p n r", n=2)))
                for a in (1, 0):
                    for n in range(2):
                        src = QT[:, T_KC + n, :].rearrange("p (m r) -> p m r", r=16)
                        dst = cx[:, n, :].rearrange("p (m r) -> p m r", r=16) if a else src
                        go(dve.tensor_tensor(dst, src, bc(peT[:, n, 16 * a:16 * a + 16].unsqueeze(1), 16, 16), ALU.add))
                    own()
                step(dve.tensor_copy(st[:, 10:11], st[:, 6:7]), "cmp_x")
                R.close(4, 1, 2)
                for qh in range(TH):
                    d = 2 * l + qh
                    index(l, qh, d)
                    attend("A", l, qh, 4 * d, lambda: best(qh))
                    attend("B", l, qh, 4 * d + 1)
                    attend("S", l, qh, 4 * d + 2)
                    if qh == 0:
                        dve.wait_ge(S["gelu_on"], l + 1)
                        for g in range(2):
                            go(dve.tensor_copy(hidc[:, g, :].rearrange("p (j n) -> p j n", n=32)[:, :, 0:NCMP],
                                               bc(gel[:, 2 + g, 0:NCMP].unsqueeze(1), 4, NCMP)))
                        own()
                        step(dve.tensor_copy(st[:, 10:11], st[:, 6:7]), "hidc_on")
                        dve.wait_ge(S["cmp_out"], l + 1)
                        step(dve.tensor_copy(kcT[:, :, 0:NCMP], cmp_k[:, :, 0:NCMP]), "cmp_sb")
                        step(dve.tensor_copy(vcr[:], cmp_v), "cmp_sb")
                    attend("W", l, qh, 4 * d + 3)
                    compressed(l, qh, d)
                step(dve.tensor_copy(st[:, 10:11], st[:, 6:7]), "branch_on")
                dve.wait_ge(S["bT_psum"], l + 1)
                step(dve.tensor_copy(QT[:, 8:12, :], psG4), "bT_dve")
                for b in range(3):
                    for t in range(2):
                        n = 2 * b + t
                        dve.wait_ge(used, R.seq + n + 1)
                        ps = psG[:, tiles[0] % 2].rearrange("p a (c t) -> p (a c) t", t=T)
                        g = zm[:, 8 * b + 4 * t:8 * b + 4 * t + 4, :]
                        m = QT[:, 12 + 4 * t:16 + 4 * t, :]
                        if b == 0:
                            go(dve.tensor_tensor(m, ps, g, ALU.mult), "tile_evac")
                        else:
                            go(dve.tensor_tensor(g, ps, g, ALU.mult), "tile_evac")
                            dve.wait_ge(S["tile_evac"], l * 27 + TILES_1 + 17 + n + 1)
                            step(dve.tensor_tensor(m, m, g, ALU.add), "dve_step")
                        tiles[0] += 1
                R.close(6)
                step(dve.tensor_copy(st[:, 10:11], st[:, 6:7]), "up_merged")
                residual()
                R.close(1)
                rest(0), rest(1)
                norm(6 + 2 * l, 5 + 2 * l, 6 + l)
                rests(4, False)
                tiles[0] += 4
                dve.wait_ge(S["tile_evac"], tiles[0])
                step(dve.tensor_tensor(pl, pl, plg, ALU.mult))
                step(dve.tensor_tensor(x[:], x[:], pl, ALU.add), "x_ready")

            dve.wait_ge(S["x_in"], 32)
            dve.wait_ge(S["consts"], N_CONSTS)
            first_layer(0)
            first_layer(1)
            tiles[0] = TILES_1
            norm(4)
            second_layer(0)
            second_layer(1)
            norm(9)


_INS = ['x', 'w_in', 'lower_bounds', 'hgrn_norm_w', 'conv_w', 'w_proj_hgrn', 'w_proj_conv', 'w_out', 'norm_mix',
        'norm_ffn', 'dense_w1', 'dense_w3', 'dense_w2', 'router_w', 'expert_w1', 'expert_w3', 'expert_w2',
        'final_norm', 'p_2', 'positions_2', 'norm_g_2', 'w_in_2', 'diff_lambda_2', 'diff_subln_g_2', 'cmp_pe_k_2',
        'cmp_w1_k_2', 'cmp_w2_k_2', 'cmp_pe_v_2', 'cmp_w1_v_2', 'cmp_w2_v_2', 'w_up_2', 'w_out_2', 'ple_norm_g_2',
        'w_ple_2', 'w_ple_gate_2', 'final_norm_g_2']
_OUTS = [((1, T, D), 'float32')]


def kernel(**inputs):
    import numpy as _np
    import concourse.bacc as _bacc
    from concourse import mybir as _mybir
    from concourse.bass_utils import run_bass_kernel_spmd as _run

    nc = _bacc.Bacc("TRN2", target_bir_lowering=False, num_devices=1, dynamic_dma_scratch_size=1024)
    arrays, args = {}, {}
    for name in _INS:
        a = _np.ascontiguousarray(inputs[name])
        arrays[f"in_{name}_dram"] = a
        args[name] = nc.dram_tensor(f"in_{name}_dram", a.shape, _mybir.dt.from_np(a.dtype), kind="ExternalInput").ap()
    outs = []
    for i, (shape, dtype) in enumerate(_OUTS):
        dt = _mybir.dt.from_np(_np.dtype(dtype))
        outs.append(nc.dram_tensor(f"out_{i}_dram", shape, dt, kind="ExternalOutput").ap())
    build(nc, args, *outs)
    r = _run(nc, [arrays], core_ids=[0])
    got = tuple(r.results[0][f"out_{i}_dram"] for i in range(len(_OUTS)))
    return got[0]
```
